# Optimizing a Trainium2 kernel written in Bass

```python
import jax, jax.numpy as jnp
from jax import lax
import numpy as np
import jax
import jax.numpy as jnp

D_MODEL = 1024
BATCH = 1
SEQ = 256
DEPTH = 2

MIX_WIDTH = D_MODEL
MLA_HEADS = 8
MLA_V = (MIX_WIDTH // 2) // MLA_HEADS
MLA_NOPE = 64
MLA_ROPE = 32
MLA_Q_LORA = D_MODEL // 4
MLA_KV_LORA = D_MODEL // 8
FOX_HEADS = 8
FOX_HEAD_DIM = (MIX_WIDTH // 2) // FOX_HEADS
FOX_W = FOX_HEADS * FOX_HEAD_DIM
IN_SPLITS = (MLA_Q_LORA, MLA_KV_LORA, MLA_ROPE, FOX_W, FOX_W, FOX_W, FOX_HEADS)
IN_COLS = sum(IN_SPLITS)
Q_BLOCK = 128
ROPE_THETA = 10000.0
D_FF = D_MODEL * 7 // 2
N_EXPERTS = 8
TOP_K = 2
EPS = 1e-6


def rms_norm(x, g):
    xf = x.astype(jnp.float32)
    y = xf * lax.rsqrt(jnp.mean(xf * xf, axis=-1, keepdims=True) + EPS)
    return (y * g.astype(jnp.float32)).astype(x.dtype)

def rope(x, positions):
    half = x.shape[-1] // 2
    inv_freq = ROPE_THETA ** (-jnp.arange(half, dtype=jnp.float32) / half)
    ang = positions.astype(jnp.float32)[..., None] * inv_freq
    cos, sin = jnp.cos(ang)[:, :, None, :], jnp.sin(ang)[:, :, None, :]
    xf = x.astype(jnp.float32)
    x1, x2 = xf[..., :half], xf[..., half:]
    return jnp.concatenate([x1 * cos - x2 * sin, x1 * sin + x2 * cos], axis=-1).astype(x.dtype)

def causal_block_attention(score_fn, v):
    B, S, H, dv = v.shape
    n_blocks = S // Q_BLOCK
    kpos = jnp.arange(S)

    def one_block(i):
        start = i * Q_BLOCK
        s = score_fn(start)
        qpos = start + jnp.arange(Q_BLOCK)
        s = jnp.where(kpos[None, :] <= qpos[:, None], s, -jnp.inf)
        p = jax.nn.softmax(s, axis=-1)
        return jnp.einsum('bhqk,bkhd->bqhd', p.astype(v.dtype), v)

    out = lax.map(one_block, jnp.arange(n_blocks))
    return out.transpose(1, 0, 2, 3, 4).reshape(B, S, H, dv)

def hybrid_mixer(h, positions, w_in, q_norm_g, w_uq, kv_norm_g, w_ukv,
                 fox_forget_b, mla_out_g, fox_out_g, w_o):
    B, S, _ = h.shape
    proj = h @ w_in
    cuts = [int(v) for v in np.cumsum(IN_SPLITS)[:-1]]
    c_q, c_kv, k_r, f_q, f_k, f_v, f_logit = jnp.split(proj, cuts, axis=-1)

    q = (rms_norm(c_q, q_norm_g) @ w_uq).reshape(B, S, MLA_HEADS, MLA_NOPE + MLA_ROPE)
    q_nope = q[..., :MLA_NOPE]
    q_rope = rope(q[..., MLA_NOPE:], positions)
    kv = (rms_norm(c_kv, kv_norm_g) @ w_ukv).reshape(B, S, MLA_HEADS, MLA_NOPE + MLA_V)
    k_nope, v_mla = kv[..., :MLA_NOPE], kv[..., MLA_NOPE:]
    k_rope = rope(k_r[:, :, None, :], positions)[:, :, 0, :]
    mla_scale = (MLA_NOPE + MLA_ROPE) ** -0.5

    def mla_scores(start):
        qn = lax.dynamic_slice_in_dim(q_nope, start, Q_BLOCK, axis=1)
        qr = lax.dynamic_slice_in_dim(q_rope, start, Q_BLOCK, axis=1)
        s = (jnp.einsum('bqhd,bkhd->bhqk', qn, k_nope, preferred_element_type=jnp.float32)
             + jnp.einsum('bqhr,bkr->bhqk', qr, k_rope, preferred_element_type=jnp.float32))
        return s * mla_scale

    o_mla = causal_block_attention(mla_scores, v_mla).reshape(B, S, MLA_HEADS * MLA_V)

    fq = f_q.reshape(B, S, FOX_HEADS, FOX_HEAD_DIM)
    fk = f_k.reshape(B, S, FOX_HEADS, FOX_HEAD_DIM)
    fv = f_v.reshape(B, S, FOX_HEADS, FOX_HEAD_DIM)
    log_f = jax.nn.log_sigmoid(f_logit.astype(jnp.float32) + fox_forget_b.astype(jnp.float32))
    F = jnp.cumsum(log_f, axis=1).transpose(0, 2, 1)
    fox_scale = FOX_HEAD_DIM ** -0.5

    def fox_scores(start):
        qb = lax.dynamic_slice_in_dim(fq, start, Q_BLOCK, axis=1)
        Fq = lax.dynamic_slice_in_dim(F, start, Q_BLOCK, axis=2)
        s = jnp.einsum('bqhd,bkhd->bhqk', qb, fk, preferred_element_type=jnp.float32)
        return s * fox_scale + Fq[..., None] - F[:, :, None, :]

    o_fox = causal_block_attention(fox_scores, fv).reshape(B, S, FOX_W)

    o = jnp.concatenate([rms_norm(o_mla, mla_out_g), rms_norm(o_fox, fox_out_g)], axis=-1)
    return o @ w_o

def swiglu(h, w_gate, w_up, w_down):
    return (jax.nn.silu(h @ w_gate) * (h @ w_up)) @ w_down

def moe_swiglu(h, router_w, w_gate, w_up, w_down):
    B, S, D = h.shape
    t = h.reshape(B * S, D)
    logits = (t @ router_w).astype(jnp.float32)
    top_v, top_i = lax.top_k(logits, TOP_K)
    top_w = jax.nn.softmax(top_v, axis=-1)
    gates = jnp.sum(jax.nn.one_hot(top_i, N_EXPERTS, dtype=jnp.float32) * top_w[..., None], axis=1)
    gates = gates.astype(t.dtype)
    y = jnp.zeros_like(t)
    for e in range(N_EXPERTS):
        y = y + gates[:, e:e + 1] * swiglu(t, w_gate[e], w_up[e], w_down[e])
    return y.reshape(B, S, D)

def modulate(h, shift, scale):
    return h * (1 + scale[:, None, :]) + shift[:, None, :]

def first_inputs(seed: int = 0) -> dict:
    key = jax.random.key(seed)
    ks = jax.random.split(key, 24)
    L, LD, LM = DEPTH, (DEPTH + 1) // 2, DEPTH // 2
    D, F, E = D_MODEL, D_FF, N_EXPERTS

    def nrm(k, shape, scale):
        return jax.random.normal(k, shape, jnp.float32) * scale

    def gain(k, shape):
        return 1.0 + 0.05 * jax.random.normal(k, shape, jnp.float32)

    positions = (jnp.arange(SEQ, dtype=jnp.int32)[None, :]
                 + jax.random.randint(ks[2], (BATCH, 1), 0, 1024, dtype=jnp.int32))
    return {
        "x": nrm(ks[0], (BATCH, SEQ, D), 1.0),
        "c": nrm(ks[1], (BATCH, D), 1.0),
        "positions": positions,
        "ada_w": nrm(ks[3], (L, D, 6 * D), 0.5 * D ** -0.5),
        "ada_b": nrm(ks[4], (L, 6 * D), 0.02),
        "attn_norm_g": gain(ks[5], (L, D)),
        "w_in": nrm(ks[6], (L, D, IN_COLS), D ** -0.5),
        "q_norm_g": gain(ks[7], (L, MLA_Q_LORA)),
        "w_uq": nrm(ks[8], (L, MLA_Q_LORA, MLA_HEADS * (MLA_NOPE + MLA_ROPE)), MLA_Q_LORA ** -0.5),
        "kv_norm_g": gain(ks[9], (L, MLA_KV_LORA)),
        "w_ukv": nrm(ks[10], (L, MLA_KV_LORA, MLA_HEADS * (MLA_NOPE + MLA_V)), MLA_KV_LORA ** -0.5),
        "fox_forget_b": jax.random.uniform(ks[11], (L, FOX_HEADS), jnp.float32, 1.0, 4.0),
        "mla_out_g": gain(ks[12], (L, MLA_HEADS * MLA_V)),
        "fox_out_g": gain(ks[13], (L, FOX_W)),
        "w_o": nrm(ks[14], (L, MIX_WIDTH, D), MIX_WIDTH ** -0.5),
        "ffn_norm_g": gain(ks[15], (L, D)),
        "dense_w_gate": nrm(ks[16], (LD, D, F), D ** -0.5),
        "dense_w_up": nrm(ks[17], (LD, D, F), D ** -0.5),
        "dense_w_down": nrm(ks[18], (LD, F, D), F ** -0.5),
        "router_w": nrm(ks[19], (LM, D, E), D ** -0.5),
        "moe_w_gate": nrm(ks[20], (LM, E, D, F), D ** -0.5),
        "moe_w_up": nrm(ks[21], (LM, E, D, F), D ** -0.5),
        "moe_w_down": nrm(ks[22], (LM, E, F, D), F ** -0.5),
        "final_norm_g": gain(ks[23], (D,)),
    }

def first_block(x, c, positions, ada_w, ada_b, attn_norm_g, w_in, q_norm_g, w_uq,
              kv_norm_g, w_ukv, fox_forget_b, mla_out_g, fox_out_g, w_o, ffn_norm_g,
              dense_w_gate, dense_w_up, dense_w_down, router_w, moe_w_gate, moe_w_up,
              moe_w_down, final_norm_g):
    c_act = jax.nn.silu(c)
    for l in range(DEPTH):
        mod = c_act @ ada_w[l] + ada_b[l]
        sh_a, sc_a, g_a, sh_f, sc_f, g_f = jnp.split(mod, 6, axis=-1)
        h = modulate(rms_norm(x, attn_norm_g[l]), sh_a, sc_a)
        mix = hybrid_mixer(h, positions, w_in[l], q_norm_g[l], w_uq[l], kv_norm_g[l],
                           w_ukv[l], fox_forget_b[l], mla_out_g[l], fox_out_g[l], w_o[l])
        x = x + g_a[:, None, :] * mix
        h = modulate(rms_norm(x, ffn_norm_g[l]), sh_f, sc_f)
        j = l // 2
        if l % 2 == 0:
            f = swiglu(h, dense_w_gate[j], dense_w_up[j], dense_w_down[j])
        else:
            f = moe_swiglu(h, router_w[j], moe_w_gate[j], moe_w_up[j], moe_w_down[j])
        x = x + g_f[:, None, :] * f
    return rms_norm(x, final_norm_g)


DEPTH_2 = 1

HEAD_DIM = 64
RWKV_HEADS = 8
RWKV_DIM = RWKV_HEADS * HEAD_DIM
LORA_W = 64
LORA_A = 64
LORA_G = 128
RWKV_COLS = 3 * RWKV_DIM + LORA_W + LORA_A + LORA_G
ATTN_PATTERNS = ((128, 1), (512, 4), (2048, 16))
ATTN_HEADS_PER_GROUP = 4
ATTN_HEADS = ATTN_HEADS_PER_GROUP * len(ATTN_PATTERNS)
ATTN_DIM = ATTN_HEADS * HEAD_DIM
ATTN_COLS = 3 * ATTN_DIM
ATTN_OUT_DIM = ATTN_HEADS_PER_GROUP * HEAD_DIM
ROT_DIM = HEAD_DIM // 4
ROPE_THETA_2 = 500000.0
N_BRANCH = 2
IN_COLS_2 = RWKV_COLS + ATTN_COLS + N_BRANCH * D_MODEL
MOE_GROUPS = 4
EXPERTS_PER_GROUP = 8
N_EXPERTS_2 = MOE_GROUPS * EXPERTS_PER_GROUP
TOP_K_INNER = 2
D_EXPERT = D_MODEL // 2
MOE_BLOCK = 128
NORM_EPS = 1e-6
GN_EPS = 64e-5


def rmsnorm(x, g, eps=NORM_EPS):
    xf = x.astype(jnp.float32)
    y = xf * lax.rsqrt(jnp.mean(xf * xf, axis=-1, keepdims=True) + eps)
    return (y * g.astype(jnp.float32)).astype(x.dtype)

def partial_rope(t, positions):
    half = ROT_DIM // 2
    inv_freq = ROPE_THETA_2 ** (-(jnp.arange(half, dtype=jnp.float32) * (2.0 / ROT_DIM)))
    ang = positions.astype(jnp.float32)[:, :, None] * inv_freq
    cos = jnp.cos(ang)[:, :, None, :]
    sin = jnp.sin(ang)[:, :, None, :]
    t1 = t[..., :half].astype(jnp.float32)
    t2 = t[..., half:ROT_DIM].astype(jnp.float32)
    rot = jnp.concatenate([t1 * cos - t2 * sin, t2 * cos + t1 * sin], axis=-1).astype(t.dtype)
    return jnp.concatenate([rot, t[..., ROT_DIM:]], axis=-1)

def wkv7_scan(r, w, k, v, a, b, reverse):
    B, T, H, N = r.shape
    seq = tuple(t.astype(jnp.float32).transpose(1, 0, 2, 3) for t in (r, w, k, v, a, b))

    def step(S, inp):
        r_t, w_t, k_t, v_t, a_t, b_t = inp
        sa = jnp.einsum('bhij,bhj->bhi', S, a_t)
        S = S * w_t[:, :, None, :] + sa[..., None] * b_t[:, :, None, :] + v_t[..., None] * k_t[:, :, None, :]
        return S, jnp.einsum('bhij,bhj->bhi', S, r_t)

    S0 = jnp.zeros((B, H, N, N), jnp.float32)
    _, y = lax.scan(step, S0, seq, reverse=reverse)
    return y.transpose(1, 0, 2, 3)

def rwkv7_branch(u, mu_prev, mu_next, w_decay0, w_decay_up, a_gate0, a_gate_up, g_up,
                 k_k, k_a, r_k, gn_w, gn_b):
    B, T, _ = u.shape
    H, N = RWKV_HEADS, HEAD_DIM
    u_prev = jnp.pad(u, ((0, 0), (1, 0), (0, 0)))[:, :T]
    u_next = jnp.pad(u, ((0, 0), (0, 1), (0, 0)))[:, 1:]
    u = u + mu_prev * (u_prev - u) + mu_next * (u_next - u)
    c = [int(i) for i in np.cumsum([0, RWKV_DIM, RWKV_DIM, RWKV_DIM, LORA_W, LORA_A, LORA_G])]
    r, k, v, xw, xa, xg = (u[..., c[i]:c[i + 1]] for i in range(6))

    def heads(t):
        return t.reshape(B, T, H, N)

    g = jax.nn.sigmoid(xg) @ g_up
    kk = heads(k * k_k).astype(jnp.float32)
    kk = kk / jnp.maximum(jnp.sqrt(jnp.sum(kk * kk, axis=-1, keepdims=True)), 1e-12)
    rh, vh = heads(r), heads(v)
    wkv = 0.0
    bonus = 0.0
    for d, reverse in enumerate((False, True)):
        w_log = -jax.nn.softplus(-(w_decay0[d] + jnp.tanh(xw) @ w_decay_up[d]).astype(jnp.float32)) - 0.5
        decay = jnp.exp(-jnp.exp(w_log))
        a = jax.nn.sigmoid(a_gate0[d] + xa @ a_gate_up[d])
        kd = heads(k * (1.0 + (a - 1.0) * k_a))
        ah = heads(a).astype(jnp.float32)
        wkv = wkv + wkv7_scan(rh, heads(decay), kd, vh, -kk, kk * ah, reverse)
        bonus = bonus + jnp.sum(rh * kd * r_k, axis=-1, keepdims=True) * vh
    mean = jnp.mean(wkv, axis=-1, keepdims=True)
    var = jnp.mean(jnp.square(wkv - mean), axis=-1, keepdims=True)
    y = ((wkv - mean) * lax.rsqrt(var + GN_EPS)).reshape(B, T, RWKV_DIM) * gn_w + gn_b
    y = y + bonus.reshape(B, T, RWKV_DIM).astype(jnp.float32)
    return (y * g).astype(u.dtype)

def banded_attention(q, k, v, band):
    B, H, L, Dh = q.shape
    nb = -(-L // band)
    Lp = nb * band
    qb = jnp.pad(q, ((0, 0), (0, 0), (0, Lp - L), (0, 0))).reshape(B, H, nb, band, Dh)

    def windows(t):
        tb = jnp.pad(t, ((0, 0), (0, 0), (band, Lp - L + band), (0, 0))).reshape(B, H, nb + 2, band, Dh)
        return jnp.concatenate([tb[:, :, :-2], tb[:, :, 1:-1], tb[:, :, 2:]], axis=3)

    kw, vw = windows(k), windows(v)
    s = jnp.einsum('bhnqd,bhnkd->bhnqk', qb, kw, preferred_element_type=jnp.float32) * (Dh ** -0.5)
    qpos = jnp.arange(nb)[:, None, None] * band + jnp.arange(band)[None, :, None]
    kpos = (jnp.arange(nb)[:, None, None] - 1) * band + jnp.arange(3 * band)[None, None, :]
    mask = (jnp.abs(kpos - qpos) <= band) & (kpos >= 0) & (kpos < L)
    s = jnp.where(mask, s, -jnp.inf)
    lse = jax.nn.logsumexp(s, axis=-1)
    p = jnp.exp(s - lse[..., None])
    o = jnp.einsum('bhnqk,bhnkd->bhnqd', p, vw.astype(jnp.float32))
    o = o.reshape(B, H, Lp, Dh)[:, :, :L].astype(v.dtype)
    return o, lse.reshape(B, H, Lp)[:, :, :L]

def dilated_window_attention(q, k, v, dilation, band):
    B, H, T, Dh = q.shape
    L = T // dilation

    def to_sub(t):
        return t.reshape(B, H, L, dilation, Dh).transpose(0, 1, 3, 2, 4).reshape(B, H * dilation, L, Dh)

    o, lse = banded_attention(to_sub(q), to_sub(k), to_sub(v), band)
    o = o.reshape(B, H, dilation, L, Dh).transpose(0, 1, 3, 2, 4).reshape(B, H, T, Dh)
    lse = lse.reshape(B, H, dilation, L).transpose(0, 1, 3, 2).reshape(B, H, T)
    return o, lse

def dilated_attention_branch(u, positions, q_norm_g, k_norm_g):
    B, T, _ = u.shape
    q = u[..., :ATTN_DIM].reshape(B, T, ATTN_HEADS, HEAD_DIM)
    k = u[..., ATTN_DIM:2 * ATTN_DIM].reshape(B, T, ATTN_HEADS, HEAD_DIM)
    v = u[..., 2 * ATTN_DIM:].reshape(B, T, ATTN_HEADS, HEAD_DIM)
    q = partial_rope(rmsnorm(q, q_norm_g), positions)
    k = partial_rope(rmsnorm(k, k_norm_g), positions)
    q, k, v = (t.transpose(0, 2, 1, 3) for t in (q, k, v))
    outs, lses = [], []
    for gi, (window, dilation) in enumerate(ATTN_PATTERNS):
        hs = slice(gi * ATTN_HEADS_PER_GROUP, (gi + 1) * ATTN_HEADS_PER_GROUP)
        o, l = dilated_window_attention(q[:, hs], k[:, hs], v[:, hs], dilation, window // (2 * dilation))
        outs.append(o)
        lses.append(l)
    alpha = jax.nn.softmax(jnp.stack(lses), axis=0)
    o = jnp.sum(alpha[..., None] * jnp.stack(outs).astype(jnp.float32), axis=0)
    return o.transpose(0, 2, 1, 3).reshape(B, T, ATTN_OUT_DIM).astype(u.dtype)

def hier_moe(h, w_router_group, b_router_group, w_router_expert, b_router_expert, w_gate, w_up, w_down):
    N, D = h.shape
    tok_idx = jnp.arange(N, dtype=jnp.int32)
    grp_logits = (h @ w_router_group).astype(jnp.float32) + b_router_group.astype(jnp.float32)
    grp_probs = jax.nn.softmax(grp_logits, axis=-1)
    grp = jnp.argmax(grp_logits, axis=-1).astype(jnp.int32)
    grp_p = grp_probs[tok_idx, grp][:, None]
    exp_logits = ((h @ w_router_expert).astype(jnp.float32)
                  + b_router_expert.astype(jnp.float32)).reshape(N, MOE_GROUPS, EXPERTS_PER_GROUP)
    exp_logits = exp_logits[tok_idx, grp]
    top_v, top_i = lax.top_k(exp_logits, TOP_K_INNER)
    gate = grp_p * jax.nn.softmax(top_v, axis=-1)
    eid = (grp[:, None] * EXPERTS_PER_GROUP + top_i).reshape(-1)
    tok = jnp.repeat(tok_idx, TOP_K_INNER)
    wts = gate.reshape(-1)
    A = N * TOP_K_INNER
    order = jnp.argsort(eid)
    e_sorted = eid[order]
    counts = jnp.bincount(eid, length=N_EXPERTS_2)
    padded = (counts + MOE_BLOCK - 1) // MOE_BLOCK * MOE_BLOCK
    pad_end = jnp.cumsum(padded)
    pad_start = pad_end - padded
    start = jnp.cumsum(counts) - counts
    dest = pad_start[e_sorted] + jnp.arange(A, dtype=jnp.int32) - start[e_sorted]
    M = (-(-A // MOE_BLOCK) + N_EXPERTS_2) * MOE_BLOCK
    n_blk = M // MOE_BLOCK
    row_tok = jnp.full((M,), N, jnp.int32).at[dest].set(tok[order])
    row_w = jnp.zeros((M,), jnp.float32).at[dest].set(wts[order])
    blk_e = jnp.minimum(jnp.searchsorted(pad_end, jnp.arange(n_blk, dtype=jnp.int32) * MOE_BLOCK, side='right'),
                        N_EXPERTS_2 - 1)
    h_pad = jnp.concatenate([h, jnp.zeros((1, D), h.dtype)], axis=0)
    xb = h_pad[row_tok].reshape(n_blk, MOE_BLOCK, D)

    def expert_block(args):
        xblk, e = args
        return (jax.nn.silu(xblk @ w_gate[e]) * (xblk @ w_up[e])) @ w_down[e]

    yb = lax.map(expert_block, (xb, blk_e)).reshape(M, D)
    y = jnp.zeros((N + 1, D), h.dtype).at[row_tok].add(yb * row_w[:, None].astype(h.dtype))
    return y[:N]

def hybrid_layer(x, positions, norm1_g, w_in, mu_prev, mu_next, w_decay0, w_decay_up, a_gate0, a_gate_up,
                 g_up, k_k, k_a, r_k, gn_w, gn_b, w_rwkv_out, q_norm_g, k_norm_g, w_attn_out, b_merge, w_out,
                 norm2_g, w_router_group, b_router_group, w_router_expert, b_router_expert, w_gate, w_up, w_down):
    B, T, D = x.shape
    h = rmsnorm(x, norm1_g)
    proj = h @ w_in
    u_rwkv = proj[..., :RWKV_COLS]
    u_attn = proj[..., RWKV_COLS:RWKV_COLS + ATTN_COLS]
    gate_logits = proj[..., RWKV_COLS + ATTN_COLS:].reshape(B, T, N_BRANCH, D) + b_merge
    y_rwkv = rwkv7_branch(u_rwkv, mu_prev, mu_next, w_decay0, w_decay_up, a_gate0, a_gate_up, g_up,
                          k_k, k_a, r_k, gn_w, gn_b) @ w_rwkv_out
    y_attn = dilated_attention_branch(u_attn, positions, q_norm_g, k_norm_g) @ w_attn_out
    gates = jax.nn.sigmoid(gate_logits)
    x = x + (gates[:, :, 0] * y_rwkv + gates[:, :, 1] * y_attn) @ w_out
    h2 = rmsnorm(x, norm2_g)
    moe = hier_moe(h2.reshape(B * T, D), w_router_group, b_router_group, w_router_expert, b_router_expert,
                   w_gate, w_up, w_down)
    return x + moe.reshape(B, T, D)

def second_inputs(seed: int = 0) -> dict:
    key = jax.random.key(seed)
    ks = iter(jax.random.split(key, 32))

    def nrm(shape, scale):
        return scale * jax.random.normal(next(ks), shape, jnp.float32)

    def unif(shape, lo, hi):
        return jax.random.uniform(next(ks), shape, dtype=jnp.float32, minval=lo, maxval=hi)

    L = DEPTH_2
    x = nrm((BATCH, SEQ, D_MODEL), 1.0)
    positions = (jnp.arange(SEQ, dtype=jnp.int32)[None, :]
                 + jax.random.randint(next(ks), (BATCH, 1), 0, 1024, dtype=jnp.int32))
    return {
        'x': x,
        'positions': positions,
        'norm1_g': 1.0 + nrm((L, D_MODEL), 0.02),
        'w_in': nrm((L, D_MODEL, IN_COLS_2), D_MODEL ** -0.5),
        'mu_prev': unif((L, RWKV_COLS), 0.0, 0.5),
        'mu_next': unif((L, RWKV_COLS), 0.0, 0.5),
        'w_decay0': unif((L, 2, RWKV_DIM), -5.0, -1.0),
        'w_decay_up': nrm((L, 2, LORA_W, RWKV_DIM), 0.5 * LORA_W ** -0.5),
        'a_gate0': nrm((L, 2, RWKV_DIM), 0.1),
        'a_gate_up': nrm((L, 2, LORA_A, RWKV_DIM), LORA_A ** -0.5),
        'g_up': nrm((L, LORA_G, RWKV_DIM), LORA_G ** -0.5),
        'k_k': 0.85 + nrm((L, RWKV_DIM), 0.05),
        'k_a': 1.0 + nrm((L, RWKV_DIM), 0.05),
        'r_k': nrm((L, RWKV_HEADS, HEAD_DIM), 0.1),
        'gn_w': 1.0 + nrm((L, RWKV_DIM), 0.02),
        'gn_b': nrm((L, RWKV_DIM), 0.02),
        'w_rwkv_out': nrm((L, RWKV_DIM, D_MODEL), RWKV_DIM ** -0.5),
        'q_norm_g': 1.0 + nrm((L, HEAD_DIM), 0.02),
        'k_norm_g': 1.0 + nrm((L, HEAD_DIM), 0.02),
        'w_attn_out': nrm((L, ATTN_OUT_DIM, D_MODEL), ATTN_OUT_DIM ** -0.5),
        'b_merge': nrm((L, N_BRANCH, D_MODEL), 0.02),
        'w_out': nrm((L, D_MODEL, D_MODEL), D_MODEL ** -0.5),
        'norm2_g': 1.0 + nrm((L, D_MODEL), 0.02),
        'w_router_group': nrm((L, D_MODEL, MOE_GROUPS), D_MODEL ** -0.5),
        'b_router_group': nrm((L, MOE_GROUPS), 0.01),
        'w_router_expert': nrm((L, D_MODEL, N_EXPERTS_2), D_MODEL ** -0.5),
        'b_router_expert': nrm((L, N_EXPERTS_2), 0.01),
        'w_gate': nrm((L, N_EXPERTS_2, D_MODEL, D_EXPERT), D_MODEL ** -0.5),
        'w_up': nrm((L, N_EXPERTS_2, D_MODEL, D_EXPERT), D_MODEL ** -0.5),
        'w_down': nrm((L, N_EXPERTS_2, D_EXPERT, D_MODEL), D_EXPERT ** -0.5),
    }

def second_block(x, positions, norm1_g, w_in, mu_prev, mu_next, w_decay0, w_decay_up, a_gate0, a_gate_up,
              g_up, k_k, k_a, r_k, gn_w, gn_b, w_rwkv_out, q_norm_g, k_norm_g, w_attn_out, b_merge, w_out,
              norm2_g, w_router_group, b_router_group, w_router_expert, b_router_expert, w_gate, w_up, w_down):
    for l in range(DEPTH_2):
        x = hybrid_layer(x, positions, norm1_g[l], w_in[l], mu_prev[l], mu_next[l], w_decay0[l], w_decay_up[l],
                         a_gate0[l], a_gate_up[l], g_up[l], k_k[l], k_a[l], r_k[l], gn_w[l], gn_b[l],
                         w_rwkv_out[l], q_norm_g[l], k_norm_g[l], w_attn_out[l], b_merge[l], w_out[l],
                         norm2_g[l], w_router_group[l], b_router_group[l], w_router_expert[l],
                         b_router_expert[l], w_gate[l], w_up[l], w_down[l])
    return x


def setup_inputs(seed=0):
    out = dict(first_inputs(seed))
    for name, value in second_inputs(seed + 1).items():
        if name != "x":
            out[name + "_2"] = value
    return out


def reference(
    x, c, positions, ada_w, ada_b, attn_norm_g, w_in, q_norm_g, w_uq, kv_norm_g, w_ukv,
    fox_forget_b, mla_out_g, fox_out_g, w_o, ffn_norm_g, dense_w_gate, dense_w_up, dense_w_down,
    router_w, moe_w_gate, moe_w_up, moe_w_down, final_norm_g, positions_2, norm1_g_2, w_in_2,
    mu_prev_2, mu_next_2, w_decay0_2, w_decay_up_2, a_gate0_2, a_gate_up_2, g_up_2, k_k_2,
    k_a_2, r_k_2, gn_w_2, gn_b_2, w_rwkv_out_2, q_norm_g_2, k_norm_g_2, w_attn_out_2, b_merge_2,
    w_out_2, norm2_g_2, w_router_group_2, b_router_group_2, w_router_expert_2,
    b_router_expert_2, w_gate_2, w_up_2, w_down_2,
):
    x = first_block(
        x, c, positions, ada_w, ada_b, attn_norm_g, w_in, q_norm_g, w_uq, kv_norm_g, w_ukv,
        fox_forget_b, mla_out_g, fox_out_g, w_o, ffn_norm_g, dense_w_gate, dense_w_up,
        dense_w_down, router_w, moe_w_gate, moe_w_up, moe_w_down, final_norm_g,
    )
    return second_block(
        x, positions_2, norm1_g_2, w_in_2, mu_prev_2, mu_next_2, w_decay0_2, w_decay_up_2,
        a_gate0_2, a_gate_up_2, g_up_2, k_k_2, k_a_2, r_k_2, gn_w_2, gn_b_2, w_rwkv_out_2,
        q_norm_g_2, k_norm_g_2, w_attn_out_2, b_merge_2, w_out_2, norm2_g_2, w_router_group_2,
        b_router_group_2, w_router_expert_2, b_router_expert_2, w_gate_2, w_up_2, w_down_2,
    )


_drawn_inputs = setup_inputs


def setup_inputs(seed=0):
    import zlib

    import numpy as np

    out = dict(_drawn_inputs(seed))
    spreads = {}
    factors = {'q_norm_g': 3.171,
     'norm1_g_2': 2.999,
     'a_gate0_2': 2.722,
     'gn_w_2': 25.458,
     'gn_b_2': 22.396,
     'q_norm_g_2': 6.99,
     'k_norm_g_2': 8.0,
     'b_merge_2': 6.474,
     'b_router_group_2': 33.715,
     'b_router_expert_2': 38.968,
     'norm2_g_2': 7.449}
    for name, (base, spread) in spreads.items():
        noise = np.random.default_rng([zlib.crc32(name.encode()), seed]).standard_normal(out[name].shape)
        drawn = base * np.exp(spread * noise) if base else spread * noise
        out[name] = jnp.asarray(drawn.astype(out[name].dtype))
    for name, factor in factors.items():
        out[name] = (out[name] * factor).astype(out[name].dtype)
    return out
```

```python
from contextlib import ExitStack, nullcontext

import numpy as np

import concourse.bass as bass
from concourse import mybir

ALU = mybir.AluOpType
ACT = mybir.ActivationFunctionType
F32 = mybir.dt.float32
I32 = mybir.dt.int32
AX = mybir.AxisListType.X

P = 128
D = 1024
DT = D // P
T = 256
TT = T // P
SLOT = 2048
RING = 14
HEADS = 8
HD = 64
EPS = 1e-6
NEG = -1e30
FFN_CHUNKS = 14
C = 64


def vector_columns():
    cols = []
    for l in range(2):
        cols += [(f"ada_b{l}", 48), (f"attn_g{l}", 8), (f"ffn_g{l}", 8), (f"q_g{l}", 2), (f"kv_g{l}", 1),
                 (f"mla_g{l}", 4), (f"fox_g{l}", 4), (f"forget_b{l}", 1)]
    cols += [("final_g", 8), ("norm1", 8), ("norm2", 8), ("mu_prev", 14), ("mu_next", 14), ("decay0", 8),
             ("gate0", 8), ("k_k", 4), ("k_a", 4), ("r_k", 4), ("gn_w", 4), ("gn_b", 4), ("qn_g", 1),
             ("kn_g", 1), ("b_merge", 16)]
    at, out = 0, {}
    for name, n in cols:
        out[name] = slice(at, at + n)
        at += n
    return out, at


def table_columns():
    cols = [("ident", 128), ("ones", 128), ("heads2", 128), ("tri", 128), ("rot1", 128), ("rot2", 128),
            ("freq1", 1), ("freq2", 1), ("causal", 128), ("iota", 128)]
    at, out = 0, {}
    for name, n in cols:
        out[name] = slice(at, at + n)
        at += n
    return out, at


STRICT, INCL, UNIT, RESET = slice(768, 832), slice(832, 896), slice(896, 960), slice(960, 1216)


def chunk_order(n):
    out = []
    for c in range(n + 1):
        if c < n:
            out += [("gate", c), ("up", c)]
        if c > 0:
            out += [("down", c - 1)]
    return out


VEC, NVEC = vector_columns()
TAB, NTAB = table_columns()


class Counter:

    def __init__(self, sem):
        self.sem, self.base, self.count = sem, 0, 0

    def up(self, k=1):
        self.count += k
        return self.sem, k

    def at(self, n):
        return self.sem, n + self.base

    def last(self):
        return self.sem, self.base + self.count

    def prime(self):
        self.base += 1

    def repeat(self, per_turn, turns):
        self.count += per_turn * (turns - 1)

    def close(self):
        self.base += self.count
        self.count = 0


class Ring:

    def __init__(self, slots, arrived, used, stream):
        self.slots, self.arrived, self.used, self.stream = slots, arrived, used, stream
        self.landed = [0] * len(slots)
        self.owner = [None] * len(slots)
        self.ordered, self.skipped = 0, 0


class Loads:

    def __init__(self, ring, n, slots=RING, turns=1):
        assert turns == 1 or n % slots == 0
        self.ring, self.n, self.slots, self.turns = ring, n, slots, turns
        self.first, self.skipped = ring.ordered, ring.skipped
        self.eager = False
        self.landed, self.owner = list(ring.landed), list(ring.owner)
        for j in range(n * turns):
            ring.owner[j % slots] = self.first + j
            ring.landed[j % slots] += 1
        ring.ordered += n * turns

    def load(self, sp, j, turn=0):
        p = j % self.slots
        at = turn * self.n + (self.first + j)
        if not isinstance(turn, int) or j >= self.slots:
            sp.wait_ge(self.ring.used, at - (self.slots - 1))
        elif self.owner[p] is not None:
            sp.wait_ge(self.ring.used, self.owner[p] + 1)
        sp.dma_start(self.ring.slots[p], self.ring.stream[at + self.skipped]).then_inc(self.ring.arrived[p], 16)

    def head(self, sp):
        for j in range(min(self.slots, self.n)):
            self.load(sp, j)

    def rest(self, sp):
        for j in range(self.slots, self.n):
            self.load(sp, j)

    def ready(self, pe, j, turn=0):
        p = j % self.slots
        per = self.n // self.slots if self.turns > 1 else 0
        pe.wait_ge(self.ring.arrived[p], turn * (16 * per) + 16 * (self.landed[p] + j // self.slots + 1))
        return self.ring.slots[p]

    def done(self, j, turn=0):
        return self.ring.used, turn * self.n + (self.first + j + 1)


class Core:

    def __init__(self, nc, ctx, dram):
        self.nc, self.dram = nc, dram
        self.counters, self.family = {}, ""
        self.ctx = ctx
        sb = self.persistent
        self.ring = sb("ring", [P, RING, SLOT])
        self.weights = self.new_ring("slot", [self.ring[:, p, :] for p in range(RING)])
        self.used = self.weights.used
        self.xT = sb("x_chan", [P, DT, T])
        self.hT = sb("h_chan", [P, DT, T])
        self.vec = sb("vec_sb", [P, NVEC])
        self.tab = sb("tab_sb", [P, NTAB])
        self.mod = sb("mod", [P, 2, 48])
        self.amp = sb("amp", [P, 2, 2, DT])
        self.rstd = sb("rstd", [P, 4, T])
        self.bank = [ctx.enter_context(nc.psum_tensor(f"bank{i}", [P, 512], F32)) for i in range(8)]
        self.posi = sb("posi", [P, T], I32)

    def persistent(self, name, shape, dt=F32):
        return self.ctx.enter_context(self.nc.sbuf_tensor(name, shape, dt))

    def new_ring(self, name, slots):
        arrived = [self.ctx.enter_context(self.nc.semaphore(f"{name}_arrived{i}")) for i in range(len(slots))]
        used = self.ctx.enter_context(self.nc.semaphore(f"{name}s_used"))
        return Ring(slots, arrived, used, self.dram["stream"])

    def counter(self, name):
        name = self.family + name
        if name not in self.counters:
            self.counters[name] = Counter(self.ctx.enter_context(self.nc.semaphore(name)))
        return self.counters[name]

    def close(self):
        for s in self.counters.values():
            s.close()

    def v(self, name, i=None):
        s = VEC[name]
        if i is None:
            return self.vec[:, s]
        return self.vec[:, s.start + i:s.start + i + 1]

    def t(self, name):
        return self.tab[:, TAB[name]]


def spread(ap, n):
    return ap.unsqueeze(1).broadcast_to([ap.shape[0], n, ap.shape[1]])


def spread_last(ap, n):
    return ap.unsqueeze(2).broadcast_to([ap.shape[0], ap.shape[1], n])


def linker(eng, sig):
    def link(ins):
        ins.then_inc(*sig.up())
        eng.wait_ge(*sig.last())
    return link


def dve_modulation(k, dve, loads, slots, l, c_row, product, link):
    for j in slots:
        w = loads.ready(dve, j)
        for i in range(2):
            at = 2 * j + i
            mul = k.nc.vector.tensor_tensor_reduce(product, w[:, i * D:(i + 1) * D], c_row, 1.0, 0.0, ALU.mult,
                                                   ALU.add, accum_out=k.mod[:, l, at:at + 1])
            if i == 0:
                link(mul)
            else:
                mul.then_inc(loads.ring.used, 1)
                dve.wait_ge(*loads.done(j))


def dve_gains(k, l, link):
    link(k.nc.vector.tensor_tensor(k.mod[:, l, :], k.mod[:, l, :], k.v(f"ada_b{l}"), ALU.add))
    for n, g in enumerate((f"attn_g{l}", f"ffn_g{l}")):
        link(k.nc.vector.scalar_tensor_tensor(k.amp[:, l, n, :], k.mod[:, l, 24 * n + 8:24 * n + 16], 1.0, k.v(g),
                                              ALU.add, ALU.mult))


def stage_setup(k, loads, nxt):
    nc = k.nc
    small = k.counter("small_arrived")
    act_step = k.counter("act_step")
    c_row, product = (k.hT[:, i:i + 4, :].rearrange("p t n -> p (t n)") for i in (0, 4))
    with nc.Block() as block:
        @block.sync
        def _(sp):
            sp.dma_start(c_row, k.dram["c_row"].partition_broadcast(P)).then_inc(*small.up(16))
            sp.dma_start(k.vec[:, :], k.dram["vec"][:, :]).then_inc(*small.up(16))
            loads.head(sp)
            sp.dma_start(k.tab[:, :], k.dram["tab"][:, :]).then_inc(*k.counter("x_arrived").up(16))
            sp.dma_start(k.xT[:, :, :], k.dram["xT"][:, :, :]).then_inc(*k.counter("x_arrived").up(16))
            loads.rest(sp)
            nxt.head(sp)

        @block.scalar
        def _(act):
            act.wait_ge(*small.at(32))
            nc.scalar.activation(c_row, c_row, ACT.Silu).then_inc(*act_step.up())

        @block.vector
        def _(dve):
            link = linker(dve, k.counter("dve_step"))
            dve.wait_ge(*act_step.at(1))
            dve_modulation(k, dve, loads, range(24), 0, c_row, product, link)
            dve_gains(k, 0, link)
    k.close()


class Norms:

    def __init__(self, k, square, groups, bank, lead="ones", count=None):
        self.k, self.square, self.groups, self.bank = k, square, groups, bank
        self.sq_ready, self.sum_ready = k.counter("squares_ready"), k.counter("sums_ready")
        self.var_ready, self.root_ready = k.counter("var_ready"), k.counter("root_ready")

    def act_squares(self, act):
        at = 0
        for src, n, _ in self.groups:
            self.k.nc.scalar.activation(self.square[:, at:at + n, :], src, ACT.Square).then_inc(*self.sq_ready.up())
            at += n

    def pe_sums(self, pe):
        k, at = self.k, 0
        for g, (_, n, _) in enumerate(self.groups):
            pe.wait_ge(*self.sq_ready.at(g + 1))
            for t in range(n):
                mm = k.nc.tensor.matmul(self.bank[g][:, 0:T], k.t("ones"),
                                        self.square[:, at + t, :], start=(t == 0), stop=(t == n - 1))
            mm.then_inc(*self.sum_ready.up())
            at += n

    def dve_var(self, dve, eps=EPS):
        k = self.k
        for g, (_, _, width) in enumerate(self.groups):
            dve.wait_ge(*self.sum_ready.at(g + 1))
            k.nc.vector.tensor_scalar(k.rstd[:, g, :], self.bank[g][:, 0:T],
                                      1.0 / width, eps, ALU.mult, ALU.add).then_inc(*k.counter("dve_step").up())
            dve.wait_ge(*k.counter("dve_step").last())
            k.nc.vector.reciprocal(k.rstd[:, g, :], k.rstd[:, g, :]).then_inc(*self.var_ready.up())

    def act_root(self, act):
        n = len(self.groups)
        act.wait_ge(*self.var_ready.at(n))
        self.k.nc.scalar.activation(self.k.rstd[:, 0:n, :], self.k.rstd[:, 0:n, :], ACT.Sqrt)\
            .then_inc(*self.root_ready.up())


def dve_modulate(k, dve, link, norms, dst, amp, shift):
    nc = k.nc
    dve.wait_ge(*norms.root_ready.at(1))
    link(nc.vector.tensor_tensor(dst[:, :, :], k.xT[:, :, :], spread(k.rstd[:, 0, :], DT), ALU.mult))
    for t in range(DT):
        b = None if shift is None else shift[:, t:t + 1]
        ops = (ALU.mult,) if shift is None else (ALU.mult, ALU.add)
        nc.vector.tensor_scalar(dst[:, t, :], dst[:, t, :], amp[:, t:t + 1], b, *ops)\
            .then_inc(*k.counter("h_ready").up())


def slot_tiles(w):
    return w.rearrange("p (t m) -> p t m", t=DT)


def stage_mixer(k, l, loads, nxt):
    nc = k.nc
    S = k.counter
    dve_step, act_step = S("dve_step"), S("act_step")
    tile_done, tile_out = S("tile_done"), S("tile_out")
    with ExitStack() as ctx:
        def sb(name, shape, dt=F32):
            return ctx.enter_context(nc.sbuf_tensor(f"{name}{l}", shape, dt))

        qm, km = sb("qm", [P, HEADS, T]), sb("km", [P, HEADS, T])
        qf, kf = sb("qf", [P, HEADS, T]), sb("kf", [P, HEADS, T])
        vm, vf = sb("vm", [P, TT, 512]), sb("vf", [P, TT, 512])
        cos, sin = sb("cos", [P, T]), sb("sin", [P, T])
        score = sb("score", [P, 2, HEADS * T])
        pT = sb("pT", [P, 2, HEADS, P])
        latent = pT[:, 0, :, :].rearrange("p h n -> p (h n)").rearrange("p (t n) -> p t n", t=4)
        cq, ckv, misc = latent[:, 0:2, :], latent[:, 2:3, :], latent[:, 3, :]
        sums = sb("sums", [P, 2, 3 * HEADS])
        oT = k.hT

        norms = Norms(k, score[:, 0, :].rearrange("p (t n) -> p t n", t=DT), [(k.xT[:, :, :], DT, D)], [k.bank[0]])
        banks = k.bank[1:7]
        NB = len(banks)
        with nc.Block() as block:
            @block.sync
            def _(sp):
                sp.dma_start(k.posi[:, :], k.dram["pos1"].partition_broadcast(P)).then_inc(*S("small_arrived").up(16))
                loads.rest(sp)

            @block.scalar
            def _(act):
                if l == 0:
                    act.wait_ge(*S("x_arrived").at(0))
                norms.act_squares(act)
                norms.act_root(act)

            @block.tensor
            def _(pe):
                norms.pe_sums(pe)
                n = 0
                for j in range(8):
                    w = slot_tiles(loads.ready(pe, j))
                    for m in range(2):
                        b = banks[n % NB]
                        if n >= NB:
                            pe.wait_ge(*tile_out.at(n - NB + 1))
                        for t in range(DT):
                            if n == 0:
                                pe.wait_ge(*S("h_ready").at(t + 1))
                            if j < 6:
                                mm = nc.tensor.matmul(b[:, 0:T], w[:, t, m * P:(m + 1) * P], k.hT[:, t, :],
                                                      start=(t == 0), stop=(t == DT - 1))
                            else:
                                mm = nc.tensor.matmul(b[:, 0:T], k.hT[:, t, m * P:(m + 1) * P], w[:, t, :],
                                                      start=(t == 0), stop=(t == DT - 1))
                        mm.then_inc(*(tile_done.up() if m == 0 else (k.used, 1)))
                        n += 1

            @block.vector
            def _(dve):
                link = linker(dve, dve_step)
                norms.dve_var(dve)
                dve_modulate(k, dve, link, norms, k.hT, k.amp[:, l, 0, :], k.mod[:, l, 0:8])
                for n in range(16):
                    b = banks[n % NB]
                    dve.wait_ge(*(tile_done.at(n // 2 + 1) if n % 2 == 0 else loads.done(n // 2)))
                    if n < 4:
                        dst = (cq[:, 0, :], cq[:, 1, :], ckv[:, 0, :], misc[:, :])[n]
                        nc.vector.tensor_copy(dst, b[:, 0:T]).then_inc(*tile_out.up())
                    elif n < 12:
                        dst, scale = (qf, HD ** -0.5) if n < 8 else (kf, 1.0)
                        h = 2 * ((n - 4) % 4)
                        nc.vector.tensor_scalar(dst[0:64, h, :], b[0:64, 0:T], scale, None, ALU.mult)
                        nc.vector.tensor_scalar(dst[0:64, h + 1, :], b[64:128, 0:T], scale, None, ALU.mult)\
                            .then_inc(*tile_out.up())
                    else:
                        half, tok = (n - 12) // 2, n % 2
                        nc.vector.tensor_copy(vf[:, tok, half * T:half * T + T], b[:, 0:T]).then_inc(*tile_out.up())
        k.close()

        sq3 = score[:, 0, :].rearrange("p (t n) -> p t n", t=DT)
        norms = Norms(k, sq3, [(cq[:, :, :], 2, 256), (ckv[:, :, :], 1, 128)], [k.bank[0], k.bank[7]])
        scratch = score[:, 1, :].rearrange("p (t n) -> p t n", t=DT)
        head_done, head_out = S("tile_done"), S("tile_out")
        rot_done, lat_ready, rope_ready = S("rot_done"), S("h_ready"), S("rope_ready")
        forget_step, forget_moved = S("forget_step"), S("forget_moved")
        with nc.Block() as block:
            @block.sync
            def _(sp):
                sp.wait_ge(*S("pool_step").at(2))
                sp.wait_ge(*forget_step.at(4))
                sp.dma_start(qf[64:65, :, :], scratch[0:8, 6, :]).then_inc(*forget_moved.up(16))
                sp.dma_start(kf[96:97, :, :], scratch[0:8, 7, :]).then_inc(*forget_moved.up(16))
                sp.wait_ge(*forget_moved.at(32))

            @block.scalar
            def _(act):
                norms.act_squares(act)
                norms.act_root(act)
                act.wait_ge(*S("angle_ready").at(1))
                nc.scalar.activation(sin[:, :], sin[:, :], ACT.Sin)
                nc.scalar.activation(cos[:, :], cos[:, :], ACT.Sin).then_inc(*S("trig_ready").up())
                act.wait_ge(*forget_step.at(1))
                nc.scalar.activation(scratch[0:8, 5, :], scratch[0:8, 5, :], ACT.Exp, scale=-1.0)\
                    .then_inc(*act_step.up())
                act.wait_ge(*act_step.last())
                nc.scalar.activation(scratch[0:8, 5, :], scratch[0:8, 5, :], ACT.Ln, bias=1.0)\
                    .then_inc(*forget_step.up())

            @block.tensor
            def _(pe):
                norms.pe_sums(pe)
                wq = loads.ready(pe, 8).rearrange("p (t h m) -> p t h m", t=2, h=HEADS)
                pe.wait_ge(*lat_ready.at(3))
                n = 0
                for h in range(HEADS):
                    b = k.bank[1 + n % 4]
                    if n >= 4:
                        pe.wait_ge(*head_out.at(n - 3))
                    for t in range(2):
                        mm = nc.tensor.matmul(b[0:96, 0:T], wq[:, t, h, 0:96], cq[:, t, :], start=(t == 0),
                                              stop=(t == 1))
                    mm.then_inc(*(head_done.up() if h < HEADS - 1 else (k.used, 1)))
                    n += 1
                wk = loads.ready(pe, 9)
                for h in range(HEADS):
                    b = k.bank[1 + n % 4]
                    pe.wait_ge(*head_out.at(n - 3))
                    nc.tensor.matmul(b[0:64, 0:T], wk[:, h * HD:(h + 1) * HD], ckv[:, 0, :], start=True, stop=True)\
                        .then_inc(*head_done.up())
                    n += 1
                for t in range(TT):
                    b = k.bank[1 + n % 4]
                    pe.wait_ge(*head_out.at(n - 3))
                    nc.tensor.matmul(b[:, :], ckv[:, 0, t * P:(t + 1) * P], wk[:, 512:1024], start=True, stop=True)\
                        .then_inc(*(head_done.up() if t == 0 else (k.used, 1)))
                    n += 1
                for i in range(5):
                    b = k.bank[5 + i % 3]
                    if i >= 3:
                        pe.wait_ge(*rope_ready.at(i - 2))
                    if i == 0:
                        pe.wait_ge(*head_out.at(8))
                    if i == 2:
                        pe.wait_ge(*norms.var_ready.at(2))
                    src = qm[64:96, 2 * i:2 * i + 2, :] if i < 4 else misc[64:96, :]
                    nc.tensor.matmul(b[64:96, 0:512 if i < 4 else T], k.t("rot1")[64:96, 64:96], src, start=True,
                                     stop=True).then_inc(*rot_done.up())

            @block.gpsimd
            def _(pool):
                nc.gpsimd.memset(qf[64:96, :, :], 0.0)
                nc.gpsimd.memset(kf[64:96, :, :], 0.0).then_inc(*S("pool_step").up())
                pool.wait_ge(*S("pool_step").at(1))
                nc.gpsimd.memset(qf[96:97, :, :], 1.0)
                nc.gpsimd.memset(kf[64:65, :, :], 1.0).then_inc(*S("pool_step").up())

            @block.vector
            def _(dve):
                link = linker(dve, dve_step)
                z, lo, e, F, negF = (scratch[0:8, i, :] for i in (3, 4, 5, 6, 7))
                link(nc.vector.tensor_scalar(z, misc[0:8, :], k.v(f"forget_b{l}")[0:8, :], None, ALU.add))
                link(nc.vector.tensor_scalar(lo, z, 0.0, None, ALU.min))
                nc.vector.scalar_tensor_tensor(e, z, 0.0, lo, ALU.max, ALU.subtract).then_inc(*forget_step.up())
                dve.wait_ge(*S("small_arrived").at(0))
                dve_angles(k, link, cos, sin, scratch[:, 0, :], scratch[:, 1, :], k.t("freq1"))
                nc.vector.tensor_copy(scratch[:, 2, :], cos[:, :]).then_inc(*S("angle_ready").up())
                norms.dve_var(dve)
                dve.wait_ge(*norms.root_ready.at(1))
                for t in range(2):
                    nc.vector.scalar_tensor_tensor(cq[:, t, :], cq[:, t, :], k.v(f"q_g{l}", t), k.rstd[:, 0, :],
                                                   ALU.mult, ALU.mult).then_inc(*lat_ready.up())
                nc.vector.scalar_tensor_tensor(ckv[:, 0, :], ckv[:, 0, :], k.v(f"kv_g{l}", 0), k.rstd[:, 1, :],
                                               ALU.mult, ALU.mult).then_inc(*lat_ready.up())
                dve.wait_ge(*forget_step.at(2))
                link(nc.vector.tensor_tensor(lo, lo, e, ALU.subtract))
                nc.vector.tensor_tensor_scan(F, k.t("ones")[0:8, 0:1].broadcast_to([8, T]), lo, 0.0, ALU.mult,
                                             ALU.add).then_inc(*forget_step.up())
                dve.wait_ge(*forget_step.at(3))
                nc.vector.tensor_scalar(negF, F, -1.0, None, ALU.mult).then_inc(*forget_step.up())
                n = 0
                for h in range(HEADS):
                    dve.wait_ge(*(head_done.at(h + 1) if h < HEADS - 1 else loads.done(8)))
                    nc.vector.tensor_scalar(qm[0:96, h, :], k.bank[1 + n % 4][0:96, 0:T], 96 ** -0.5, None,
                                            ALU.mult).then_inc(*head_out.up())
                    n += 1
                for h in range(HEADS):
                    dve.wait_ge(*head_done.at(n))
                    nc.vector.tensor_copy(km[0:64, h, :], k.bank[1 + n % 4][0:64, 0:T]).then_inc(*head_out.up())
                    n += 1
                for t in range(TT):
                    dve.wait_ge(*(head_done.at(n) if t == 0 else loads.done(9)))
                    nc.vector.tensor_copy(vm[:, t, :], k.bank[1 + n % 4][:, :]).then_inc(*head_out.up())
                    n += 1
                dve.wait_ge(*S("trig_ready").at(1))
                dve.wait_ge(*head_out.at(8))
                for i in range(5):
                    dve.wait_ge(*rot_done.at(i + 1))
                    b = k.bank[5 + i % 3]
                    if i < 4:
                        swapped = b[64:96, :].rearrange("p (h n) -> p h n", h=2)
                        x = qm[64:96, 2 * i:2 * i + 2, :]
                        turned = scratch[64:96, 3:5, :]
                        link(nc.vector.tensor_tensor(turned, swapped, spread(sin[64:96, :], 2), ALU.mult))
                        link(nc.vector.tensor_tensor(x, x, spread(cos[64:96, :], 2), ALU.mult))
                        nc.vector.tensor_tensor(x, x, turned, ALU.add).then_inc(*rope_ready.up())
                        dve.wait_ge(*rope_ready.last())
                    else:
                        turned, own = scratch[64:96, 3, :], scratch[64:96, 4, :]
                        link(nc.vector.tensor_tensor(turned, b[64:96, 0:T], sin[64:96, :], ALU.mult))
                        link(nc.vector.tensor_tensor(own, misc[64:96, :], cos[64:96, :], ALU.mult))
                        nc.vector.tensor_tensor(km[64:96, :, :], spread(own, HEADS), spread(turned, HEADS), ALU.add)
        k.close()

        units = [(kind, qb) for kind in range(2) for qb in range(TT)]
        causal_attention(k, units, ((qm, km, vm, 96), (qf, kf, vf, 97)), score, pT, sums, oT)

        norms = Norms(k, score[:, 0, :].rearrange("p (t n) -> p t n", t=DT),
                      [(oT[:, 0:4, :], 4, 512), (oT[:, 4:8, :], 4, 512)], [k.bank[0], k.bank[7]])
        out_ready = S("h_ready")
        with nc.Block() as block:
            @block.sync
            def _(sp):
                nxt.head(sp)

            @block.scalar
            def _(act):
                norms.act_squares(act)
                norms.act_root(act)

            @block.tensor
            def _(pe):
                norms.pe_sums(pe)
                project_square(k, pe, loads, 10, oT, out_ready, DT)

            @block.vector
            def _(dve):
                norms.dve_var(dve)
                dve.wait_ge(*norms.root_ready.at(1))
                for t in range(DT):
                    g = k.v(f"mla_g{l}", t) if t < 4 else k.v(f"fox_g{l}", t - 4)
                    nc.vector.scalar_tensor_tensor(oT[:, t, :], oT[:, t, :], g, k.rstd[:, t // 4, :], ALU.mult,
                                                   ALU.mult).then_inc(*out_ready.up())
                for n in range(8):
                    dve.wait_ge(*project_square_done(k, loads, 10, n))
                    nc.vector.scalar_tensor_tensor(k.xT[:, n, :], k.bank[1 + n % 4][:, 0:T],
                                                   k.mod[:, l, 16 + n:17 + n], k.xT[:, n, :], ALU.mult,
                                                   ALU.add).then_inc(*S("tile_out").up())
        k.close()


def project_square(k, pe, loads, j0, src, src_ready, kt):
    for n in range(8):
        if n % 2 == 0:
            w = slot_tiles(loads.ready(pe, j0 + n // 2))
        b = k.bank[1 + n % 4]
        if n >= 4:
            pe.wait_ge(*k.counter("tile_out").at(n - 3))
        for t in range(kt):
            if n == 0:
                pe.wait_ge(*src_ready.at(t + 1))
            mm = k.nc.tensor.matmul(b[:, 0:T], w[:, t, (n % 2) * P:(n % 2) * P + P], src[:, t, :], start=(t == 0),
                                    stop=(t == kt - 1))
        mm.then_inc(*(k.counter("tile_done").up() if n % 2 == 0 else (k.used, 1)))


def project_square_done(k, loads, j0, n):
    return k.counter("tile_done").at(n // 2 + 1) if n % 2 == 0 else loads.done(j0 + n // 2)


def dve_angles(k, link, cos, sin, a, r, freq):
    v = k.nc.vector
    link(v.tensor_copy(a, k.posi[:, :]))
    link(v.tensor_scalar(a, a, freq, None, ALU.mult))
    link(v.tensor_scalar(r, a, float(1 / (2 * np.pi)), 12582912.0, ALU.mult, ALU.add))
    link(v.tensor_scalar(r, r, -12582912.0, None, ALU.add))
    parts = (6.28125, 0.0019350051879882812, 2 * np.pi - 6.28125 - 0.0019350051879882812)
    for part in parts:
        link(v.scalar_tensor_tensor(a, r, -float(part), a, ALU.mult, ALU.add))
    link(v.tensor_scalar(sin[:, :], a, 3.1415925, -3.1415925, ALU.min, ALU.max))
    link(v.tensor_scalar(r, sin[:, :], -1.0, None, ALU.mult))
    link(v.tensor_tensor(r, r, sin[:, :], ALU.max))
    link(v.tensor_scalar(cos[:, :], r, -1.0, float(np.pi / 2), ALU.mult, ALU.add))


def causal_attention(k, units, kinds, score, pT, sums, oT):
    nc = k.nc
    S = k.counter
    scores_done, scores_out, max_ready = S("tile_done"), S("tile_out"), S("max_ready")
    exp_done, prob_ready = S("exp_done"), S("prob_ready")
    turn_done, turn_out, o_done, o_out = S("turn_done"), S("turn_out"), S("o_done"), S("o_out")
    N = len(units)
    batches = [0]
    for _, qb in units:
        batches.append(batches[-1] + 2 * (qb + 1))
    s4 = [score[:, i, :].rearrange("p (h n) -> p h n", h=HEADS) for i in range(2)]
    with nc.Block() as block:
        @block.tensor
        def _(pe):
            def scores(u):
                kind, qb = units[u]
                q, kk, _, rows = kinds[kind]
                nk = P * (qb + 1)
                if u >= 1:
                    pe.wait_ge(*scores_out.at(u))
                for h in range(HEADS):
                    mm = nc.tensor.matmul(k.bank[h // 2][:, (h % 2) * T:(h % 2) * T + nk],
                                          q[0:rows, h, qb * P:(qb + 1) * P], kk[0:rows, h, 0:nk], start=True,
                                          stop=True)
                mm.then_inc(*scores_done.up())

            scores(0)
            for u, (kind, qb) in enumerate(units):
                if u + 1 < N:
                    scores(u + 1)
                v = kinds[kind][2]
                pe.wait_ge(*prob_ready.at(u + 1))
                for b in range(batches[u], batches[u + 1]):
                    kb, h0 = (b - batches[u]) // 2, 4 * ((b - batches[u]) % 2)
                    if b >= 2:
                        pe.wait_ge(*turn_out.at(b - 1))
                    for i in range(4):
                        mm = nc.tensor.transpose(k.bank[4 + b % 2][:, i * P:(i + 1) * P],
                                                 s4[u % 2][:, h0 + i, kb * P:(kb + 1) * P], k.t("ident"))
                    mm.then_inc(*turn_done.up())
                pe.wait_ge(*turn_out.at(batches[u + 1]))
                if u >= 2:
                    pe.wait_ge(*o_out.at(u - 1))
                for h in range(HEADS):
                    half = 64 * (h % 2)
                    for kb in range(qb + 1):
                        mm = nc.tensor.matmul(k.bank[6 + u % 2][half:half + 64, (h // 2) * P:(h // 2) * P + P],
                                              v[:, kb, h * HD:(h + 1) * HD], pT[:, kb, h, :], start=(kb == 0),
                                              stop=(kb == qb))
                mm.then_inc(*o_done.up())

        @block.scalar
        def _(act):
            for u, (_, qb) in enumerate(units):
                act.wait_ge(*max_ready.at(u + 1))
                for h in range(HEADS):
                    e = nc.scalar.activation(s4[u % 2][:, h, 0:P * (qb + 1)], s4[u % 2][:, h, 0:P * (qb + 1)],
                                             ACT.Exp, bias=sums[:, u % 2, h:h + 1],
                                             accum_out=sums[:, u % 2, 8 + h:9 + h])
                e.then_inc(*exp_done.up())

        @block.vector
        def _(dve):
            link = linker(dve, S("dve_step"))

            def masked(u):
                _, qb = units[u]
                s = s4[u % 2]
                if u >= 2:
                    dve.wait_ge(*turn_done.at(batches[u - 1]))
                dve.wait_ge(*scores_done.at(u + 1))
                for b in range(4):
                    ps = k.bank[b][:, :].rearrange("p (h n) -> p h n", h=2)
                    if qb:
                        nc.vector.tensor_copy(s[:, 2 * b:2 * b + 2, 0:P], ps[:, :, 0:P])
                    last = nc.vector.tensor_tensor(s[:, 2 * b:2 * b + 2, qb * P:(qb + 1) * P],
                                                   ps[:, :, qb * P:(qb + 1) * P], spread(k.t("causal"), 2), ALU.add)
                last.then_inc(*scores_out.up())
                dve.wait_ge(*scores_out.last())
                nc.vector.tensor_reduce(sums[:, u % 2, 0:8], s[:, :, 0:P * (qb + 1)], AX, ALU.max, negate=True)\
                    .then_inc(*max_ready.up())

            def finish(u):
                _, qb = units[u]
                nk = P * (qb + 1)
                dve.wait_ge(*exp_done.at(u + 1))
                inv = sums[:, u % 2, 16:24]
                link(nc.vector.reciprocal(inv, sums[:, u % 2, 8:16]))
                nc.vector.tensor_tensor(s4[u % 2][:, :, 0:nk], s4[u % 2][:, :, 0:nk], spread_last(inv, nk),
                                        ALU.mult).then_inc(*prob_ready.up())
                for b in range(batches[u], batches[u + 1]):
                    kb, h0 = (b - batches[u]) // 2, 4 * ((b - batches[u]) % 2)
                    if b == batches[u] and u >= 1:
                        dve.wait_ge(*o_done.at(u))
                    dve.wait_ge(*turn_done.at(b + 1))
                    nc.vector.tensor_copy(pT[:, kb, h0:h0 + 4, :],
                                          k.bank[4 + b % 2][:, :].rearrange("p (h n) -> p h n", h=4))\
                        .then_inc(*turn_out.up())
                kind = units[u][0]
                dve.wait_ge(*o_done.at(u + 1))
                nc.vector.tensor_copy(oT[:, 4 * kind:4 * kind + 4, qb * P:(qb + 1) * P],
                                      k.bank[6 + u % 2][:, :].rearrange("p (t n) -> p t n", t=4))\
                    .then_inc(*o_out.up())

            for u in range(N + 1):
                if u < N:
                    masked(u)
                if u >= 1:
                    finish(u - 1)
    k.close()


def stage_dense(k, l, loads, nxt):
    nc = k.nc
    S = k.counter
    pairs = chunk_order(FFN_CHUNKS)
    where = {key: j for j, key in enumerate(pairs)}
    silu_done, hidden_ready, hidden_used = S("silu_done"), S("hidden_ready"), S("hidden_used")
    with ExitStack() as ctx:
        def sb(name, shape):
            return ctx.enter_context(nc.sbuf_tensor(name, shape, F32))

        square = sb("dense_square", [P, DT, T])
        silu = sb("dense_silu", [P, 2, 2, T])
        hidden = sb("dense_hidden", [P, 2, 2, T])
        c_row, product = sb("ada_c", [P, D]), sb("ada_product", [P, D])
        side_slots = sb("ada_slots", [P, 3, SLOT])
        side_ring = k.new_ring("ada_slot", [side_slots[:, i, :] for i in range(3)])
        side_ring.skipped = 24
        side = Loads(side_ring, 24, 3)
        norms = Norms(k, square, [(k.xT[:, :, :], DT, D)], [k.bank[0]])
        with nc.Block() as block:
            @block.sync
            def _(sp):
                sp.dma_start(c_row[:, :], k.dram["c_row"].partition_broadcast(P))\
                    .then_inc(*S("small_arrived").up(16))
                side.head(sp)
                for j in range(loads.slots, loads.n):
                    loads.load(sp, j)
                    done = j - loads.slots + 1
                    for i in range((done - 1) * 3 // 4, done * 3 // 4):
                        side.load(sp, side.slots + i)
                nxt.head(sp)

            @block.scalar
            def _(act):
                norms.act_squares(act)
                norms.act_root(act)
                act.wait_ge(*S("small_arrived").at(16))
                nc.scalar.activation(c_row[:, :], c_row[:, :], ACT.Silu).then_inc(*S("act_step").up())
                for c in range(FFN_CHUNKS):
                    act.wait_ge(*loads.done(where["gate", c]))
                    if c >= 2:
                        act.wait_ge(*hidden_ready.at(c - 1))
                    nc.scalar.activation(silu[:, c % 2, :, :], k.bank[4 + c % 2][:, :].rearrange(
                        "p (t n) -> p t n", t=2), ACT.Silu).then_inc(*silu_done.up())

            @block.tensor
            def _(pe):
                norms.pe_sums(pe)
                pe.wait_ge(*norms.var_ready.at(1))
                for j, (kind, c) in enumerate(pairs):
                    w = loads.ready(pe, j)
                    if kind == "down":
                        pe.wait_ge(*hidden_ready.at(c + 1))
                        w = w.rearrange("p (f n) -> p f n", f=2)
                        for f in range(2):
                            for t in range(DT):
                                mm = nc.tensor.matmul(k.bank[t // 2][:, (t % 2) * T:(t % 2) * T + T],
                                                      w[:, f, t * P:(t + 1) * P], hidden[:, c % 2, f, :],
                                                      start=(c == 0 and f == 0 and t % 2 == 0),
                                                      stop=(c == FFN_CHUNKS - 1 and f == 1),
                                                      skip_group_check=True)
                        mm.then_inc(k.used, 1)
                        continue
                    b = k.bank[(4 if kind == "gate" else 6) + c % 2]
                    if c >= 2:
                        pe.wait_ge(*(silu_done if kind == "gate" else hidden_ready).at(c - 1))
                    w = slot_tiles(w)
                    for f in range(2):
                        for t in range(DT):
                            if j == 0 and f == 0:
                                pe.wait_ge(*S("h_ready").at(t + 1))
                            mm = nc.tensor.matmul(b[:, f * T:(f + 1) * T], w[:, t, f * P:(f + 1) * P], k.hT[:, t, :],
                                                  start=(t == 0), stop=(t == DT - 1))
                    mm.then_inc(k.used, 1)

            @block.vector
            def _(dve):
                link = linker(dve, S("dve_step"))
                norms.dve_var(dve)
                dve_modulate(k, dve, link, norms, k.hT, k.amp[:, l, 1, :], k.mod[:, l, 24:32])
                for c in range(FFN_CHUNKS):
                    dve.wait_ge(*loads.done(where["up", c]))
                    dve.wait_ge(*silu_done.at(c + 1))
                    if c >= 2:
                        dve.wait_ge(*loads.done(where["down", c - 2]))
                    nc.vector.tensor_tensor(hidden[:, c % 2, :, :], silu[:, c % 2, :, :],
                                            k.bank[6 + c % 2][:, :].rearrange("p (t n) -> p t n", t=2),
                                            ALU.mult).then_inc(*hidden_ready.up())
                    if c == 0:
                        dve.wait_ge(*S("act_step").at(1))
                    dve_modulation(k, dve, side, range(2 * c, min(2 * c + 2, 24)), l + 1, c_row[:, :],
                                   product[:, :], link)
                dve_gains(k, l + 1, link)
                dve.wait_ge(*loads.done(len(pairs) - 1))
                for t in range(DT):
                    nc.vector.scalar_tensor_tensor(k.xT[:, t, :], k.bank[t // 2][:, (t % 2) * T:(t % 2) * T + T],
                                                   k.mod[:, l, 40 + t:41 + t], k.xT[:, t, :], ALU.mult, ALU.add)\
                        .then_inc(*S("dve_step").up())
        k.close()


def stage_route(k, m, norm_gain, shift):
    nc = k.nc
    S = k.counter
    E, W, R = m.experts, m.width, m.router_cols
    dve_step, pe_step, act_step = S("dve_step"), S("pe_step"), S("act_step")
    norms = Norms(k, m.square, [(k.xT[:, :, :], DT, D)], [k.bank[0]])
    small = m.small

    def col(name, n=None):
        return small[name][:, :, :] if n is None else small[name][:, :, 0:n]

    with nc.Block() as block:
        @block.sync
        def _(sp):
            sp.dma_start(m.router_w[:, :, :], k.dram[m.router_name][:, :, :]).then_inc(*S("small_arrived").up(16))
            if m.grouped:
                sp.dma_start(m.router_b[:, :], k.dram["router_b"].partition_broadcast(P))\
                    .then_inc(*S("small_arrived").up(16))

        @block.scalar
        def _(act):
            norms.act_squares(act)
            norms.act_root(act)
            act.wait_ge(*S("logit_step").at(1))
            nc.scalar.activation(col("w"), col("w"), ACT.Exp).then_inc(*S("exp_done").up())
            if m.grouped:
                act.wait_ge(*S("logit_step").at(2))
                nc.scalar.activation(col("gl"), col("gl"), ACT.Exp).then_inc(*S("exp_done").up())

        @block.tensor
        def _(pe):
            norms.pe_sums(pe)
            pe.wait_ge(*S("h_ready").at(DT))
            pe.wait_ge(*S("small_arrived").last())
            for tok in range(TT):
                for t in range(DT):
                    mm = nc.tensor.matmul(k.bank[1][:, tok * R:(tok + 1) * R], k.hT[:, t, tok * P:(tok + 1) * P],
                                          m.router_w[:, t, :], start=(t == 0), stop=(t == DT - 1))
            mm.then_inc(*pe_step.up())
            for n in range(4):
                tok, q = n // 2, n % 2
                b = k.bank[2 + n % 2]
                if n >= 2:
                    pe.wait_ge(*S("turn_out").at(n - 1))
                for i in range(4):
                    mm = nc.tensor.transpose(b[:, i * P:(i + 1) * P], k.hT[:, 4 * q + i, tok * P:(tok + 1) * P],
                                             k.t("ident"))
                mm.then_inc(*S("turn_done").up())
            pe.wait_ge(*S("mask_ready").at(1))
            nc.tensor.matmul(k.bank[4][:, 0:E], k.t("tri"), m.chosen[:, 0, :], start=True, stop=True)
            nc.tensor.matmul(k.bank[4][:, E:2 * E], k.t("ones"), m.chosen[:, 0, :], start=True, stop=False)
            nc.tensor.matmul(k.bank[4][:, E:2 * E], k.t("tri"), m.chosen[:, 1, :], start=False, stop=True)
            nc.tensor.matmul(k.bank[4][:, 2 * E:3 * E], k.t("ones"), m.chosen[:, 0, :], start=True, stop=False)
            nc.tensor.matmul(k.bank[4][:, 2 * E:3 * E], k.t("ones"), m.chosen[:, 1, :], start=False, stop=True)\
                .then_inc(*pe_step.up())

        @block.vector
        def _(dve):
            link = linker(dve, dve_step)
            v = nc.vector
            norms.dve_var(dve)
            dve_modulate(k, dve, link, norms, k.hT, norm_gain, shift)
            link(v.memset(m.acc[:, :, :], 0.0))
            dve.wait_ge(*pe_step.at(1))
            logit = k.bank[1][:, 0:TT * R].rearrange("p (t e) -> p t e", t=TT)
            iota = spread(k.t("iota")[:, 0:E], TT)
            L = col("l", E)

            def first_max(src, n, top, hot, rest):
                link(v.tensor_reduce(top, src, AX, ALU.max))
                link(v.tensor_tensor(hot, src, top.broadcast_to([P, TT, n]), ALU.is_equal))
                idx = col("idx", n)
                link(v.tensor_scalar(idx, hot, -1e6, 1e6, ALU.mult, ALU.add))
                link(v.tensor_tensor(idx, idx, iota[:, :, 0:n], ALU.add))
                link(v.tensor_reduce(col("at"), idx, AX, ALU.min))
                link(v.tensor_tensor(hot, iota[:, :, 0:n], col("at").broadcast_to([P, TT, n]), ALU.is_equal))
                if rest is not None:
                    link(v.scalar_tensor_tensor(rest, hot, 2 * NEG, src, ALU.mult, ALU.add))

            if m.grouped:
                bias = m.router_b[:, :]
                G, per = 4, E // 4
                gl, ghot = col("gl"), col("ghot")
                link(v.tensor_tensor(gl, logit[:, :, 0:G], spread(bias[:, 0:G], TT), ALU.add))
                link(v.tensor_tensor(L, logit[:, :, G:], spread(bias[:, G:], TT), ALU.add))
                first_max(gl, G, col("m0"), ghot, None)
                v.tensor_tensor(gl, gl, col("m0").broadcast_to([P, TT, G]), ALU.subtract).then_inc(*dve_step.up())
                for tok in range(TT):
                    link(v.tensor_tensor(small["hot1"][:, tok, 0:E].rearrange("p (g e) -> p g e", g=G),
                                         spread_last(small["ghot"][:, tok, :], per),
                                         spread_last(small["ghot"][:, tok, :], per), ALU.mult))
                link(v.tensor_tensor(L, L, col("hot1", E), ALU.mult))
                link(v.tensor_scalar(col("hot1", E), col("hot1", E), -NEG, NEG, ALU.mult, ALU.add))
                link(v.tensor_tensor(L, L, col("hot1", E), ALU.add))
            else:
                link(v.tensor_copy(L, logit))
            first_max(L, E, col("m1"), col("hot1", E), col("l2", E))
            first_max(col("l2", E), E, col("m2"), col("hot2", E), None)
            v.tensor_tensor(col("w"), col("m2"), col("m1"), ALU.subtract).then_inc(*S("logit_step").up())
            if m.grouped:
                dve.wait_ge(*S("logit_step").at(1))
                v.tensor_scalar(col("at"), col("m1"), 0.0, None, ALU.mult).then_inc(*S("logit_step").up())
            v.tensor_tensor(m.chosen[:, :, :], col("hot1", E), col("hot2", E), ALU.add).then_inc(*S("mask_ready").up())
            dve.wait_ge(*S("exp_done").at(1))
            link(v.tensor_scalar(col("w1"), col("w"), 1.0, None, ALU.add))
            if m.grouped:
                dve.wait_ge(*S("exp_done").at(2))
                link(v.tensor_reduce(col("gs"), col("gl"), AX, ALU.add))
                link(v.tensor_tensor(col("w1"), col("w1"), col("gs"), ALU.mult))
            link(v.reciprocal(col("w1"), col("w1")))
            link(v.tensor_tensor(col("w"), col("w"), col("w1"), ALU.mult))
            link(v.tensor_tensor(col("hot1", E), col("hot1", E), col("w1").broadcast_to([P, TT, E]), ALU.mult))
            link(v.tensor_tensor(col("hot2", E), col("hot2", E), col("w").broadcast_to([P, TT, E]), ALU.mult))
            link(v.tensor_tensor(m.gates[:, :, :], col("hot1", E), col("hot2", E), ALU.add))
            for n in range(4):
                tok, q = n // 2, n % 2
                dve.wait_ge(*S("turn_done").at(n + 1))
                v.tensor_copy(m.h_tok[:, tok, q * 512:(q + 1) * 512], k.bank[2 + n % 2][:, :])\
                    .then_inc(*S("turn_out").up())
            dve.wait_ge(*pe_step.at(2))
            dve.wait_ge(*S("mask_ready").at(1))
            link(v.tensor_tensor(m.place[:, :, :], k.bank[4][:, 0:2 * E].rearrange("p (t e) -> p t e", t=TT),
                                 m.chosen[:, :, :], ALU.mult))
            link(v.tensor_scalar(m.place[:, :, :], m.place[:, :, :], -1.0, None, ALU.add))
            link(v.tensor_reduce(m.fullest[:, 0:1], k.bank[4][:, 2 * E:3 * E], AX, ALU.max))
            link(v.tensor_copy(m.fullest_int[:, :], m.fullest[:, 0:1]))
    k.close()


def build_dve(k, m, dve, later):
    nc = k.nc
    S = k.counter
    E, W = m.experts, m.width
    G = E * W // P
    link = linker(dve, S("dve_step"))
    v = nc.vector
    pick = [m.pick[:, t, 0:E * W].rearrange("p (e w) -> p e w", e=E) for t in range(TT)]
    for t in range(TT):
        if later:
            link(v.tensor_scalar(m.place[:, t, :], m.place[:, t, :], -float(W), None, ALU.add))
        link(v.tensor_tensor(pick[t], spread(k.t("iota")[:, 0:W], E), spread_last(m.place[:, t, :], W),
                             ALU.is_equal))
        if t > 0:
            dve.wait_ge(*S("turn_done").at(t * (G // 4)))
        v.tensor_tensor(m.gated[:, :].rearrange("p (e w) -> p e w", e=E), pick[t],
                        spread_last(m.gates[:, t, :], W), ALU.mult).then_inc(*S("mask_ready").up())
        for b in range(G // 4):
            n = t * (G // 4) + b
            dve.wait_ge(*S("turn_done").at(n + 1))
            v.tensor_copy(m.gate_t[:, 4 * b:4 * b + 4, t * P:(t + 1) * P],
                          k.bank[n % 4][:, :].rearrange("p (g n) -> p g n", g=4)).then_inc(*S("turn_out").up())
    v.memset(m.pick[:, :, E * W:E * W + P], 0.0).then_inc(*S("picks_ready").up())


def build_pe(k, m, pe):
    nc = k.nc
    S = k.counter
    G = m.experts * m.width // P
    for t in range(TT):
        pe.wait_ge(*S("mask_ready").at(t + 1))
        for b in range(G // 4):
            n = t * (G // 4) + b
            if n >= 4:
                pe.wait_ge(*S("turn_out").at(n - 3))
            for i in range(4):
                mm = nc.tensor.transpose(k.bank[n % 4][:, i * P:(i + 1) * P],
                                         m.gated[:, (4 * b + i) * P:(4 * b + i + 1) * P], k.t("ident"))
            mm.then_inc(*S("turn_done").up())


def stage_experts(k, m, loads, nxt, later=False, when=lambda eng: nullcontext()):
    nc = k.nc
    S = k.counter
    W = m.width
    per_group = P // W
    chunks = m.chunks * per_group
    G = m.experts // per_group
    order = chunk_order(chunks)
    where = {key: j for j, key in enumerate(order)}
    xg, silu, hidden, y = m.xg, m.silu, m.hidden, m.y
    picked, xg_ready = S("picked"), S("xg_ready")
    silu_done, hidden_ready = S("silu_done"), S("hidden_ready")
    y_ready = S("y_ready")
    spread_done, acc_done = S("spread_done"), S("acc_done")
    primed = [silu_done, hidden_ready, y_ready, spread_done, acc_done]
    for c in primed:
        c.prime()

    with nc.Block() as block:
        @block.sync
        def _(sp):
            with when(sp):
                if loads.eager:
                    loads.head(sp)
                loads.rest(sp)
                with sp.Fori(1, G) as g:
                    for j in range(loads.n):
                        loads.load(sp, j, g)
                if nxt is not None:
                    nxt.head(sp)

        @block.tensor
        def _(pe):
            with when(pe):
                def gather(g):
                    for half in range(2):
                        for i in range(4):
                            for t in range(TT):
                                mm = nc.tensor.matmul(k.bank[6 + half][:, i * P:(i + 1) * P],
                                                      m.h_tok[:, t, (4 * half + i) * P:(4 * half + i + 1) * P],
                                                      m.pick[:, t, bass.ds(g * P, P)] if not isinstance(g, int) else
                                                      m.pick[:, t, g * P:(g + 1) * P],
                                                      start=(t == 0), stop=(t == TT - 1))
                        mm.then_inc(*picked.up())

                build_pe(k, m, pe)
                pe.wait_ge(*S("picks_ready").at(1))
                gather(0)
                with pe.Fori(0, G) as g:
                    pe.wait_ge(*xg_ready.at(g * 2 + 2))
                    for j, (kind, c) in enumerate(order):
                        w = loads.ready(pe, j, g)
                        e = c // m.chunks
                        if kind == "down":
                            pe.wait_ge(*hidden_ready.at(g * chunks + (c + 1)))
                            if c == 0:
                                pe.wait_ge(*y_ready.at(g * 2))
                            w = w.rearrange("p (f n) -> p f n", f=2)
                            for f in range(2):
                                for half in range(2):
                                    mm = nc.tensor.matmul(
                                        k.bank[half][e * W:(e + 1) * W, :], hidden[:, c % 2, f, :],
                                        w[:, f, half * 512:(half + 1) * 512],
                                        start=(c % m.chunks == 0 and f == 0),
                                        stop=(c % m.chunks == m.chunks - 1 and f == 1))
                            mm.then_inc(loads.ring.used, 1)
                            continue
                        b = k.bank[(2 if kind == "gate" else 4) + c % 2]
                        pe.wait_ge(*(silu_done if kind == "gate" else hidden_ready).at(g * chunks + (c - 1)))\
                            if c >= 2 else pe.wait_ge(*(silu_done if kind == "gate" else hidden_ready).at(g * chunks))
                        w = slot_tiles(w)
                        for f in range(2):
                            for t in range(DT):
                                mm = nc.tensor.matmul(b[:, f * W:(f + 1) * W], w[:, t, f * P:(f + 1) * P],
                                                      xg[:, t, e * W:(e + 1) * W], start=(t == 0), stop=(t == DT - 1))
                        mm.then_inc(loads.ring.used, 1)
                    pe.wait_ge(*acc_done.at(g * 4 + 0))
                    gather(g + 1)
                    pe.wait_ge(*y_ready.at(g * 2 + 2))
                    for q in range(4):
                        if q < 2:
                            pe.wait_ge(*xg_ready.at(g * 2 + (3 + q)))
                        else:
                            pe.wait_ge(*acc_done.at(g * 4 + (q - 1)))
                        for i in range(2):
                            mm = nc.tensor.matmul(k.bank[6 + q % 2][:, i * T:(i + 1) * T],
                                                  y[:, (2 * q + i) * P:(2 * q + i + 1) * P],
                                                  m.gate_t[:, bass.ds(g, 1), :], start=True, stop=True)
                        mm.then_inc(*spread_done.up())
                picked.count += 2 * (G - 1)
                spread_done.count += 4 * (G - 1)

        @block.scalar
        def _(act):
            with when(act):
                with act.Fori(0, G) as g:
                    for c in range(chunks):
                        act.wait_ge(*loads.done(where["gate", c], g))
                        act.wait_ge(*hidden_ready.at(g * chunks + max(c - 1, 0)))
                        nc.scalar.activation(silu[:, c % 2, :, :], k.bank[2 + c % 2][:, 0:2 * W].rearrange(
                            "p (f n) -> p f n", f=2), ACT.Silu).then_inc(*silu_done.up())
                silu_done.repeat(chunks, G)

        @block.vector
        def _(dve):
            with when(dve):
                v = nc.vector

                def take(g):
                    for half in range(2):
                        dve.wait_ge(*picked.at(g * 2 + (half + 1)))
                        if half == 0 and not isinstance(g, int):
                            dve.wait_ge(*loads.done(loads.n - 1, g - 1))
                        v.tensor_copy(xg[:, 4 * half:4 * half + 4, :],
                                      k.bank[6 + half][:, :].rearrange("p (t n) -> p t n", t=4)).then_inc(*xg_ready.up())

                for i, c in enumerate(primed):
                    nc.vector.memset(m.mark[:, i:i + 1], 0.0).then_inc(c.sem, 1)
                build_dve(k, m, dve, later)
                take(0)
                with dve.Fori(0, G) as g:
                    for c in range(chunks):
                        dve.wait_ge(*loads.done(where["up", c], g))
                        dve.wait_ge(*silu_done.at(g * chunks + (c + 1)))
                        if c >= 2:
                            dve.wait_ge(*loads.done(where["down", c - 2], g))
                        v.tensor_tensor(hidden[:, c % 2, :, :], silu[:, c % 2, :, :],
                                        k.bank[4 + c % 2][:, 0:2 * W].rearrange("p (f n) -> p f n", f=2),
                                        ALU.mult).then_inc(*hidden_ready.up())
                    dve.wait_ge(*loads.done(where["down", chunks - 1], g))
                    for half in range(2):
                        if half == 0:
                            dve.wait_ge(*spread_done.at(g * 4))
                        v.tensor_copy(y[:, half * 512:(half + 1) * 512], k.bank[half][:, :]).then_inc(*y_ready.up())
                    take(g + 1)
                    for q in range(4):
                        dve.wait_ge(*spread_done.at(g * 4 + (q + 1)))
                        v.tensor_tensor(m.acc[:, 2 * q:2 * q + 2, :],
                                        k.bank[6 + q % 2][:, :].rearrange("p (t n) -> p t n", t=2),
                                        m.acc[:, 2 * q:2 * q + 2, :], ALU.add).then_inc(*acc_done.up())
                hidden_ready.repeat(chunks, G)
                y_ready.repeat(2, G)
                acc_done.repeat(4, G)
                xg_ready.count += 2 * (G - 1)
    k.close()


class Mixture:

    def __init__(self, k, ctx, name, experts, width, chunks, router_name, router_cols, grouped, lent):
        self.name = name
        self.experts, self.width, self.chunks = experts, width, chunks
        self.router_name, self.router_cols, self.grouped = router_name, router_cols, grouped

        def sb(n, shape, dt=F32):
            return ctx.enter_context(k.nc.sbuf_tensor(f"{name}_{n}", shape, dt))

        E = experts
        self.router_w = sb("router_w", [P, DT, router_cols])
        self.router_b = sb("router_b", [P, router_cols])
        self.chosen, self.gates, self.place = (sb(n, [P, TT, E]) for n in ("chosen", "gates", "place"))
        self.fullest, self.fullest_int = sb("fullest", [P, 1]), sb("fullest_int", [P, 1], I32)
        self.mark = sb("mark", [1, 8])
        self.small = {n: sb(n, [P, TT, E]) for n in ("l", "l2", "hot1", "hot2", "idx")}
        self.small.update({n: sb(n, [P, TT, 1]) for n in ("m0", "m1", "m2", "at", "w", "w1", "gs")})
        self.small.update({n: sb(n, [P, TT, 4]) for n in ("gl", "ghot")})
        self.pick = sb("pick", [P, TT, E * width + P])
        shared = sb("shared", [P, 2 * D])
        self.gated = shared[:, 0:E * width]
        self.gate_t = sb("gate_t", [P, E * width // P, T])
        self.h_tok = sb("h_tok", [P, TT, D])
        self.acc = sb("acc", [P, DT, T])
        self.xg = shared[:, 0:D].rearrange("p (t n) -> p t n", t=DT)
        self.silu, self.hidden = sb("silu", [P, 2, 2, width]), sb("hidden", [P, 2, 2, width])
        self.y = shared[:, D:2 * D]
        self.square = self.acc
        self.spare_slots = [k.ring[:, p, :] for p in lent]
        if len(lent) < 3:
            self.spare_slots.append(sb("spare", [P, SLOT])[:, :])


def stage_mixture(k, m, gain, shift, loads, nxt, residual_gate):
    nc = k.nc
    stage_route(k, m, gain, shift)
    stage_experts(k, m, loads, nxt)
    fullest = nc.values_load(m.fullest_int[0:1, 0:1], min_val=0, max_val=T)
    k.family = m.name + "_more_"
    ring = k.new_ring(k.family + "slot", m.spare_slots)
    for r in range(1, -(-T // m.width)):
        ring.skipped = loads.first + loads.skipped - ring.ordered
        again = Loads(ring, loads.n, len(m.spare_slots), loads.turns)
        again.eager = True
        stage_experts(k, m, again, None, True, lambda eng: eng.If(fullest > r * m.width))
    k.family = ""
    with nc.Block() as block:
        @block.vector
        def _(dve):
            for t in range(DT):
                if residual_gate is None:
                    ins = nc.vector.tensor_tensor(k.xT[:, t, :], m.acc[:, t, :], k.xT[:, t, :], ALU.add)
                else:
                    ins = nc.vector.scalar_tensor_tensor(k.xT[:, t, :], m.acc[:, t, :], residual_gate[:, t:t + 1],
                                                         k.xT[:, t, :], ALU.mult, ALU.add)
                ins.then_inc(*k.counter("dve_step").up())
    k.close()


HYBRID_RING = 12


def head_slice(half):
    return slice(half * HD, half * HD + HD)


def stage_hybrid(k, loads, nxt):
    nc = k.nc
    S = k.counter
    with ExitStack() as ctx:
        def sb(name, shape, dt=F32):
            return ctx.enter_context(nc.sbuf_tensor(f"hyb_{name}", shape, dt))

        u = sb("u", [P, 14, T + 2])
        gate = sb("gate", [P, 16, T])
        work = sb("work", [P, 3, SLOT])
        g = sb("g", [P, 4, T])
        tab2, whole, v_back = sb("tab2", [P, 1216]), sb("whole", [P, 8, C]), sb("v_back", [P, 4, T])
        lent = k.ring[:, HYBRID_RING:RING, :].rearrange("p s n -> p (s n)")
        acc = k.hT
        flat = work[:, :, :].rearrange("p s n -> p (s n)")
        qk = flat[:, 0:3072].rearrange("p (t n) -> p t n", t=12)
        v_tok = flat[:, 3072:4608].rearrange("p (t n) -> p t n", t=2)
        dilated = flat[:, 4608:6144].rearrange("p (q n) -> p q n", q=2)

        stage_final_norm(k)
        hybrid_project(k, loads, u, gate, qk, v_tok, dilated, tab2, lent)
        hybrid_qk(k, qk, lent)
        hybrid_attention(k, qk, v_tok, dilated, lent, g)
        hybrid_merge(k, loads, None, 1, g[:, 0:2, :], gate, acc)
        rec = Recurrence(k, u, g, tab2, flat, whole, v_back)
        rec.prepare(loads)
        rec.scan(loads)
        rec.finish()
        hybrid_merge(k, loads, nxt, 0, rec.y, gate, acc)


def stage_final_norm(k):
    nc = k.nc
    norms = Norms(k, k.hT, [(k.xT[:, :, :], DT, D)], [k.bank[0]])
    with nc.Block() as block:
        @block.scalar
        def _(act):
            norms.act_squares(act)
            norms.act_root(act)

        @block.tensor
        def _(pe):
            norms.pe_sums(pe)

        @block.vector
        def _(dve):
            link = linker(dve, k.counter("dve_step"))
            norms.dve_var(dve)
            dve_modulate(k, dve, link, norms, k.xT, k.v("final_g"), None)
    k.close()


def hybrid_project(k, loads, u, gate, qk, v_tok, dilated, tab2, lent):
    nc = k.nc
    S = k.counter
    tile_done, tile_out, gate_out = S("tile_done"), S("tile_out"), S("gate_out")
    norms = Norms(k, lent[:, 0:2048].rearrange("p (t n) -> p t n", t=DT), [(k.xT[:, :, :], DT, D)], [k.bank[0]])
    banks = k.bank[1:8]
    NB = len(banks)
    with nc.Block() as block:
        @block.sync
        def _(sp):
            sp.dma_start(k.posi[:, :], k.dram["pos2"].partition_broadcast(P)).then_inc(*S("small_arrived").up(16))
            sp.dma_start(dilated, k.dram["dilated"][:, :, :]).then_inc(*S("small_arrived").up(16))
            sp.dma_start(tab2[:, :], k.dram["tab2"][:, :]).then_inc(*S("small_arrived").up(16))
            loads.rest(sp)

        @block.scalar
        def _(act):
            norms.act_squares(act)
            norms.act_root(act)
            for n in range(32, 48):
                act.wait_ge(*(tile_done.at(n // 2 + 1) if n % 2 == 0 else loads.done(n // 2)))
                nc.scalar.activation(gate[:, n - 32, :], banks[n % NB][:, 0:T], ACT.Sigmoid,
                                     bias=k.v("b_merge", n - 32)).then_inc(*gate_out.up())

        @block.tensor
        def _(pe):
            norms.pe_sums(pe)
            for n in range(48):
                if n % 2 == 0:
                    w = slot_tiles(loads.ready(pe, n // 2))
                b = banks[n % NB]
                if n >= NB:
                    before = n - NB
                    pe.wait_ge(*(tile_out.at(before + 1) if before < 32 else gate_out.at(before - 31)))
                for t in range(DT):
                    if n == 0:
                        pe.wait_ge(*S("h_ready").at(t + 1))
                    m = n % 2
                    lhsT, rhs = w[:, t, m * P:(m + 1) * P], k.hT[:, t, :]
                    if 26 <= n < 32:
                        lhsT, rhs = k.hT[:, t, m * P:(m + 1) * P], w[:, t, :]
                    mm = nc.tensor.matmul(b[:, 0:T], lhsT, rhs, start=(t == 0), stop=(t == DT - 1))
                mm.then_inc(*(tile_done.up() if n % 2 == 0 else (k.used, 1)))

        @block.vector
        def _(dve):
            link = linker(dve, S("dve_step"))
            nc.vector.memset(u[:, :, 0:1], 0.0)
            nc.vector.memset(u[:, :, T + 1:T + 2], 0.0)
            norms.dve_var(dve)
            dve_modulate(k, dve, link, norms, k.hT, k.v("norm1"), None)
            for n in range(32):
                dve.wait_ge(*(tile_done.at(n // 2 + 1) if n % 2 == 0 else loads.done(n // 2)))
                if n < 14:
                    dst = u[:, n, 1:T + 1]
                elif n < 26:
                    dst = qk[:, n - 14, :]
                else:
                    dst = v_tok[:, n % 2, ((n - 26) // 2) * T:((n - 26) // 2) * T + T]
                nc.vector.tensor_copy(dst, banks[n % NB][:, 0:T]).then_inc(*tile_out.up())
    k.close()


def hybrid_qk(k, qk, lent):
    nc = k.nc
    S = k.counter
    sq = lent[:, 0:3072].rearrange("p (t n) -> p t n", t=12)
    cos, sin = lent[:, 3072:3328], lent[:, 3328:3584]
    a, r = lent[:, 3584:3840], lent[:, 3840:4096]
    with nc.Block() as block:
        @block.scalar
        def _(act):
            nc.scalar.activation(sq, qk, ACT.Square).then_inc(*S("squares_ready").up())
            act.wait_ge(*S("angle_ready").at(1))
            nc.scalar.activation(sin, sin, ACT.Sin)
            nc.scalar.activation(cos, cos, ACT.Sin).then_inc(*S("trig_ready").up())
            act.wait_ge(*S("var_ready").at(1))
            nc.scalar.activation(sq, sq, ACT.Sqrt).then_inc(*S("root_ready").up())

        @block.tensor
        def _(pe):
            pe.wait_ge(*S("squares_ready").at(1))
            for j in range(6):
                nc.tensor.matmul(k.bank[j][:, :], k.t("heads2"), sq[:, 2 * j:2 * j + 2, :], start=True, stop=True)\
                    .then_inc(*S("sums_ready").up())
            for j in range(6):
                pe.wait_ge(*S("h_ready").at(j // 3 + 1))
                nc.tensor.matmul(k.bank[j][:, :], k.t("rot2"), qk[:, 2 * j:2 * j + 2, :], start=True, stop=True)\
                    .then_inc(*S("rot_done").up())

        @block.vector
        def _(dve):
            v = nc.vector
            link = linker(dve, S("dve_step"))
            dve_angles(k, link, cos, sin, a, r, k.t("freq2"))
            v.tensor_copy(a, cos).then_inc(*S("angle_ready").up())
            for j in range(6):
                dve.wait_ge(*S("sums_ready").at(j + 1))
                link(v.tensor_scalar(sq[:, 2 * j:2 * j + 2, :], k.bank[j][:, :].rearrange("p (t n) -> p t n", t=2),
                                     1.0 / HD, EPS, ALU.mult, ALU.add))
            v.reciprocal(sq, sq).then_inc(*S("var_ready").up())
            dve.wait_ge(*S("root_ready").at(1))
            for i, g in enumerate(("qn_g", "kn_g")):
                half = slice(6 * i, 6 * i + 6)
                v.scalar_tensor_tensor(qk[:, half, :], qk[:, half, :], k.v(g, 0), sq[:, half, :], ALU.mult,
                                       ALU.mult).then_inc(*S("h_ready").up())
            dve.wait_ge(*S("h_ready").at(2))
            dve.wait_ge(*S("trig_ready").at(1))
            for j in range(6):
                pair = slice(2 * j, 2 * j + 2)
                dve.wait_ge(*S("rot_done").at(j + 1))
                link(v.tensor_tensor(sq[:, pair, :], k.bank[j][:, :].rearrange("p (t n) -> p t n", t=2),
                                     spread(sin, 2), ALU.mult))
                link(v.tensor_tensor(qk[:, pair, :], qk[:, pair, :], spread(cos, 2), ALU.mult))
                link(v.tensor_tensor(qk[:, pair, :], qk[:, pair, :], sq[:, pair, :], ALU.add))
    k.close()


def hybrid_attention(k, qk, v_tok, dilated, lent, out):
    nc = k.nc
    S = k.counter
    units = [(qb, hs) for qb in range(TT) for hs in range(4)]
    N = len(units)
    score = [lent[:, i * 768:(i + 1) * 768] for i in range(2)]
    pT = lent[:, 1536:2304].rearrange("p (i n) -> p i n", i=6)
    sums = lent[:, 2304:2312]
    with nc.Block() as block:
        @block.tensor
        def _(pe):
            def scores(i):
                qb, hs = units[i]
                rows = head_slice(hs % 2)
                if i >= 1:
                    pe.wait_ge(*S("tile_out").at(i))
                for w in range(3):
                    t = (4 * w + hs) // 2
                    b = k.bank[w // 2]
                    mm = nc.tensor.matmul(b[:, (w % 2) * T:(w % 2) * T + T], qk[rows, t, qb * P:(qb + 1) * P],
                                          qk[rows, 6 + t, :], start=True, stop=True)
                mm.then_inc(*S("tile_done").up())

            scores(0)
            for i, (qb, hs) in enumerate(units):
                if i + 1 < N:
                    scores(i + 1)
                pe.wait_ge(*S("prob_ready").at(i + 1))
                if i >= 1:
                    pe.wait_ge(*S("turn_out").at(i))
                for j in range(6):
                    mm = nc.tensor.transpose(k.bank[2 + j // 3][:, (j % 3) * P:(j % 3 + 1) * P],
                                             score[i % 2][:, j * P:(j + 1) * P], k.t("ident"))
                mm.then_inc(*S("turn_done").up())
                pe.wait_ge(*S("turn_out").at(i + 1))
                half = head_slice(hs % 2)
                if i >= 2:
                    pe.wait_ge(*S("o_out").at(i - 1))
                for j in range(6):
                    w, kb = j // 2, j % 2
                    mm = nc.tensor.matmul(k.bank[4 + i % 2][half, 0:P],
                                          v_tok[:, kb, (4 * w + hs) * HD:(4 * w + hs + 1) * HD], pT[:, j, :],
                                          start=(j == 0), stop=(j == 5))
                mm.then_inc(*S("o_done").up())

        @block.scalar
        def _(act):
            for i in range(N):
                act.wait_ge(*S("max_ready").at(i + 1))
                nc.scalar.activation(score[i % 2], score[i % 2], ACT.Exp, bias=sums[:, i % 2:i % 2 + 1],
                                     accum_out=sums[:, 2 + i % 2:3 + i % 2]).then_inc(*S("exp_done").up())

        @block.vector
        def _(dve):
            v = nc.vector
            link = linker(dve, S("dve_step"))

            def masked(i):
                qb, hs = units[i]
                s = score[i % 2]
                if i >= 2:
                    dve.wait_ge(*S("turn_done").at(i - 1))
                dve.wait_ge(*S("tile_done").at(i + 1))
                v.scalar_tensor_tensor(s[:, 0:512], k.bank[0][:, :], HD ** -0.5, dilated[:, qb, 0:512], ALU.mult,
                                       ALU.add)
                v.scalar_tensor_tensor(s[:, 512:768], k.bank[1][:, 0:T], HD ** -0.5, dilated[:, qb, 512:768],
                                       ALU.mult, ALU.add).then_inc(*S("tile_out").up())
                dve.wait_ge(*S("tile_out").last())
                v.tensor_reduce(sums[:, i % 2:i % 2 + 1], s, AX, ALU.max, negate=True).then_inc(*S("max_ready").up())

            def finish(i):
                qb, hs = units[i]
                dve.wait_ge(*S("exp_done").at(i + 1))
                inv = sums[:, 4 + i % 2:5 + i % 2]
                link(v.reciprocal(inv, sums[:, 2 + i % 2:3 + i % 2]))
                v.tensor_scalar(score[i % 2], score[i % 2], inv, None, ALU.mult).then_inc(*S("prob_ready").up())
                dve.wait_ge(*S("turn_done").at(i + 1))
                if i >= 1:
                    dve.wait_ge(*S("o_done").at(i))
                for b in range(2):
                    last = v.tensor_copy(pT[:, 3 * b:3 * b + 3, :],
                                         k.bank[2 + b][:, 0:3 * P].rearrange("p (i n) -> p i n", i=3))
                last.then_inc(*S("turn_out").up())
                half = head_slice(hs % 2)
                dve.wait_ge(*S("o_done").at(i + 1))
                v.tensor_copy(out[half, hs // 2, qb * P:(qb + 1) * P], k.bank[4 + i % 2][half, 0:P])\
                    .then_inc(*S("o_out").up())

            for i in range(N + 1):
                if i < N:
                    masked(i)
                if i >= 1:
                    finish(i - 1)
    k.close()


def hybrid_merge(k, loads, nxt, branch, src, gate, acc):
    nc = k.nc
    S = k.counter
    kt = 2 if branch else 4
    with nc.Block() as block:
        @block.sync
        def _(sp):
            if nxt is not None:
                nxt.head(sp)

        @block.tensor
        def _(pe):
            for n in range(DT):
                if branch:
                    w = loads.ready(pe, 24).rearrange("p (t m) -> p t m", t=2)[:, :, n * P:(n + 1) * P]
                else:
                    w = loads.ready(pe, 26 + n // 4).rearrange("p (t m) -> p t m", t=4)[
                        :, :, (n % 4) * P:(n % 4) * P + P]
                if n >= 4:
                    pe.wait_ge(*S("tile_out").at(n - 3))
                for t in range(kt):
                    mm = nc.tensor.matmul(k.bank[n % 4][:, 0:T], w[:, t, :], src[:, t, :], start=(t == 0),
                                          stop=(t == kt - 1))
                last = n == DT - 1 if branch else n % 4 == 3
                mm.then_inc(*((k.used, 1) if last else S("tile_done").up()))
            if branch:
                return
            for n in range(DT):
                if n % 2 == 0:
                    w = slot_tiles(loads.ready(pe, 28 + n // 2))
                b = k.bank[4 + n % 4]
                if n >= 4:
                    pe.wait_ge(*S("gate_out").at(n - 3))
                for t in range(DT):
                    if n == 0:
                        pe.wait_ge(*S("h_ready").at(t + 1))
                    mm = nc.tensor.matmul(b[:, 0:T], w[:, t, (n % 2) * P:(n % 2) * P + P], acc[:, t, :],
                                          start=(t == 0), stop=(t == DT - 1))
                mm.then_inc(*(S("rot_done").up() if n % 2 == 0 else (k.used, 1)))

        @block.vector
        def _(dve):
            v = nc.vector
            for n in range(DT):
                if branch:
                    dve.wait_ge(*(S("tile_done").at(n + 1) if n < DT - 1 else loads.done(24)))
                    v.tensor_tensor(acc[:, n, :], k.bank[n % 4][:, 0:T], gate[:, 8 + n, :], ALU.mult)\
                        .then_inc(*S("tile_out").up())
                    continue
                dve.wait_ge(*(S("tile_done").at(n + 1 - n // 4) if n % 4 < 3 else loads.done(26 + n // 4)))
                v.tensor_tensor(gate[:, n, :], k.bank[n % 4][:, 0:T], gate[:, n, :], ALU.mult)\
                    .then_inc(*S("tile_out").up())
                dve.wait_ge(*S("tile_out").last())
                v.tensor_tensor(acc[:, n, :], acc[:, n, :], gate[:, n, :], ALU.add).then_inc(*S("h_ready").up())
            if branch:
                return
            for n in range(DT):
                dve.wait_ge(*(S("rot_done").at(n // 2 + 1) if n % 2 == 0 else loads.done(28 + n // 2)))
                v.tensor_tensor(k.xT[:, n, :], k.bank[4 + n % 4][:, 0:T], k.xT[:, n, :], ALU.add)\
                    .then_inc(*S("gate_out").up())
    k.close()


class Recurrence:

    def __init__(self, k, u, g, tab2, flat, whole, v_back):
        self.v_back = v_back
        self.k, self.u, self.g, self.tab2, self.flat, self.whole = k, u, g, tab2, flat, whole
        self.big = [k.ring[:, 8 + i, :].rearrange("p (n t) -> p n t", n=8) for i in range(4)]
        self.at, self.bt, self.rt, self.kt = self.big
        self.mixed = u[:, :, 1:T + 1]
        self.y = self.mixed[:, 0:4, :]
        self.bonus = self.mixed[:, 4:8, :]
        self.v = self.mixed[:, 8:12, :]

    def prepare(self, loads):
        k, u, g, flat = self.k, self.u, self.g, self.flat
        nc = k.nc
        S = k.counter
        mixed = self.mixed
        both = k.ring[:, 8:12, :].rearrange("p s n -> p (s n)")
        d_prev = both[:, 0:14 * T].rearrange("p (t n) -> p t n", t=14)
        d_next = both[:, 4096:4096 + 14 * T].rearrange("p (t n) -> p t n", t=14)
        lw, ag, L = (flat[:, i * SLOT:(i + 1) * SLOT].rearrange("p (n t) -> p n t", n=8) for i in range(3))
        kd = k.ring[:, 12, :].rearrange("p (n t) -> p n t", n=8)
        kk = k.ring[:, 13, 0:1024].rearrange("p (n t) -> p n t", n=4)
        tmp = k.ring[:, 13, 1024:2048].rearrange("p (n t) -> p n t", n=4)
        at, bt, rt, kt = self.at, self.bt, self.rt, self.kt
        r, kx, v_ = mixed[:, 0:4, :], mixed[:, 4:8, :], mixed[:, 8:12, :]
        reset = self.tab2[:, RESET]
        self.decay_end = decay_end = k.rstd[:, 0, 0:32].rearrange("p (n c) -> p n c", n=8)

        def turned(x, d):
            return x[:, :, ::-1] if d else x

        with nc.Block() as block:
            @block.scalar
            def _(act):
                act.wait_ge(*S("h_ready").at(1))
                a = nc.scalar.activation
                a(mixed[0:64, 12, :], mixed[0:64, 12, :], ACT.Tanh)
                a(mixed[:, 13, :], mixed[:, 13, :], ACT.Sigmoid).then_inc(*S("act_step").up())
                for d in range(2):
                    for i in range(4):
                        n = 4 * d + i
                        act.wait_ge(*S("tile_done").at(n + 1))
                        dst = lw[:, n, ::-1] if d else lw[:, n, :]
                        a(dst, k.bank[n % 2][:, 0:T], ACT.Sigmoid, bias=k.v("decay0", n))
                        a(ag[:, n, :], k.bank[2 + n % 2][:, 0:T], ACT.Sigmoid, bias=k.v("gate0", n))\
                            .then_inc(*S("tile_out").up())
                act.wait_ge(*S("kk_step").at(1))
                a(tmp, kk, ACT.Square).then_inc(*S("squares_ready").up())
                act.wait_ge(*S("kk_step").at(2))
                a(tmp, tmp, ACT.Sqrt).then_inc(*S("root_ready").up())
                act.wait_ge(*S("log_ready").at(1))
                a(rt, L, ACT.Exp).then_inc(*S("exp_done").up())
                a(at, at, ACT.Exp).then_inc(*S("exp_done").up())
                a(bt, L, ACT.Exp, scale=-1.0).then_inc(*S("exp_done").up())

            @block.tensor
            def _(pe):
                w = loads.ready(pe, 25)
                pe.wait_ge(*S("act_step").at(1))
                for d in range(2):
                    for i in range(4):
                        n = 4 * d + i
                        if n >= 2:
                            pe.wait_ge(*S("tile_out").at(n - 1))
                        cols = slice(d * 512 + i * P, d * 512 + (i + 1) * P)
                        nc.tensor.matmul(k.bank[n % 2][:, 0:T], w[0:64, cols], mixed[0:64, 12, :], start=True,
                                         stop=True)
                        nc.tensor.matmul(k.bank[2 + n % 2][:, 0:T], w[64:128, cols], mixed[64:128, 12, :],
                                         start=True, stop=True).then_inc(*S("tile_done").up())
                for i in range(4):
                    mm = nc.tensor.matmul(k.bank[4 + i // 2][:, (i % 2) * T:(i % 2) * T + T],
                                          w[:, 1024 + i * P:1024 + (i + 1) * P], mixed[:, 13, :], start=True,
                                          stop=True)
                mm.then_inc(k.used, 1)
                pe.wait_ge(*S("squares_ready").at(1))
                for i in range(2):
                    mm = nc.tensor.matmul(k.bank[6 + i][:, :], k.t("heads2"), tmp[:, 2 * i:2 * i + 2, :], start=True,
                                          stop=True)
                mm.then_inc(*S("sums_ready").up())
                pe.wait_ge(*S("kk_step").at(3))
                for i in range(2):
                    mm = nc.tensor.matmul(k.bank[6 + i][:, :], k.t("heads2"), tmp[:, 2 * i:2 * i + 2, :], start=True,
                                          stop=True)
                mm.then_inc(*S("sums_ready").up())

            @block.vector
            def _(dve):
                v = nc.vector
                link = linker(dve, S("dve_step"))
                v.tensor_tensor(d_prev, u[:, :, 0:T], mixed, ALU.subtract)
                link(v.tensor_tensor(d_next, u[:, :, 2:T + 2], mixed, ALU.subtract))
                for step, (d, mu) in enumerate(((d_prev, "mu_prev"), (d_next, "mu_next"))):
                    for t in range(14):
                        last = v.scalar_tensor_tensor(mixed[:, t, :], d[:, t, :], k.v(mu, t), mixed[:, t, :],
                                                      ALU.mult, ALU.add)
                    if step == 0:
                        link(last)
                last.then_inc(*S("h_ready").up())
                dve.wait_ge(*S("h_ready").at(1))
                v.tensor_copy(self.v_back[:, :, :], v_[:, :, ::-1]).then_inc(*S("dve_step").up())
                for t in range(4):
                    last = v.tensor_scalar(kk[:, t, :], kx[:, t, :], k.v("k_k", t), None, ALU.mult)
                last.then_inc(*S("kk_step").up())
                dve.wait_ge(*S("sums_ready").at(1))
                for i in range(2):
                    last = v.tensor_copy(tmp[:, 2 * i:2 * i + 2, :],
                                         k.bank[6 + i][:, :].rearrange("p (t n) -> p t n", t=2))
                last.then_inc(*S("kk_step").up())
                dve.wait_ge(*S("root_ready").at(1))
                link(v.tensor_scalar(tmp, tmp, 1e-12, None, ALU.max))
                link(v.reciprocal(tmp, tmp))
                link(v.tensor_tensor(kk, kk, tmp, ALU.mult))
                dve.wait_ge(*S("tile_out").at(8))
                for n in range(8):
                    link(v.tensor_scalar(kd[:, n, :], ag[:, n, :], -1.0, k.v("k_a", n % 4), ALU.add, ALU.mult))
                for d in range(2):
                    link(v.scalar_tensor_tensor(kd[:, 4 * d:4 * d + 4, :], kd[:, 4 * d:4 * d + 4, :], 1.0, kx,
                                                ALU.add, ALU.mult))
                link(v.tensor_tensor(tmp, kd[:, 0:4, :], kd[:, 4:8, :], ALU.add))
                for t in range(4):
                    last = v.scalar_tensor_tensor(tmp[:, t, :], tmp[:, t, :], k.v("r_k", t), r[:, t, :], ALU.mult,
                                                  ALU.mult)
                last.then_inc(*S("kk_step").up())
                link(v.tensor_scalar(lw, lw, -float(np.exp(-0.5)), None, ALU.mult))
                for n in range(8):
                    last = v.tensor_tensor_scan(L[:, n, :], reset, lw[:, n, :], 0.0, ALU.mult, ALU.add)
                link(last)
                v.tensor_tensor(at, L, lw, ALU.subtract).then_inc(*S("log_ready").up())
                dve.wait_ge(*S("exp_done").at(1))
                link(v.tensor_copy(decay_end, rt[:, :, C - 1:T:C]))
                for d in range(2):
                    link(v.tensor_tensor(rt[:, 4 * d:4 * d + 4, :], rt[:, 4 * d:4 * d + 4, :], turned(r, d),
                                         ALU.mult))
                dve.wait_ge(*S("exp_done").at(3))
                for d in range(2):
                    s = slice(4 * d, 4 * d + 4)
                    link(v.scalar_tensor_tensor(at[:, s, :], at[:, s, :], -1.0, turned(kk, d), ALU.mult, ALU.mult))
                    link(v.tensor_tensor(kt[:, s, :], bt[:, s, :], turned(kd[:, s, :], d), ALU.mult))
                    link(v.tensor_tensor(ag[:, s, :], ag[:, s, :], kk, ALU.mult))
                    link(v.tensor_tensor(bt[:, s, :], bt[:, s, :], turned(ag[:, s, :], d), ALU.mult))
                dve.wait_ge(*S("sums_ready").at(2))
                for i in range(2):
                    link(v.tensor_tensor(self.bonus[:, 2 * i:2 * i + 2, :],
                                         k.bank[6 + i][:, :].rearrange("p (t n) -> p t n", t=2),
                                         v_[:, 2 * i:2 * i + 2, :], ALU.mult))
                    link(v.tensor_copy(g[:, 2 * i:2 * i + 2, :],
                                       k.bank[4 + i][:, :].rearrange("p (t n) -> p t n", t=2)))
        k.close()

    def scan(self, loads):
        k = self.k
        nc = k.nc
        S = k.counter
        names = ["b_row", "k_row", "v_row", "low", "inv", "inv_t", "mid", "ak", "rb", "rk"]
        pool = {}
        for i, (name, s) in enumerate((name, s) for s in range(2) for name in names):
            home = self.flat[:, i * 512:(i + 1) * 512] if i < 12 else \
                k.ring[:, 12:14, :].rearrange("p s n -> p (s n)")[:, (i - 12) * 512:(i - 11) * 512]
            pool[name, s] = home.rearrange("p (n t) -> p n t", n=8)
        state = k.rstd[:, 2:4, :].rearrange("p s n -> p (s n)").rearrange("p (n t) -> p n t", n=8)
        masks = self.tab2
        at, bt, rt, kt = self.at, self.bt, self.rt, self.kt
        done, out = S("tile_done"), S("tile_out")
        chunks = T // C
        tensors = [b[:, :].rearrange("p (n t) -> p n t", n=8) for b in k.bank]
        decay_end = self.decay_end

        def masked(i):
            return masks[:, i * C:(i + 1) * C]

        def cut(x, c):
            return x[:, :, c * C:(c + 1) * C]

        ident = k.t("ident")

        def product(bank, terms):
            for n in range(8):
                for half in range(2):
                    rows = head_slice(half)
                    for i, (a, b) in enumerate(terms):
                        mm = nc.tensor.matmul(tensors[bank][rows, n, :], a(rows, n), b(rows, n), start=(i == 0),
                                              stop=(i == len(terms) - 1))
            mm.then_inc(*done.up())

        def of(x):
            return lambda rows, n: x[rows, n, :]

        def own(rows, n):
            return ident[rows, rows]

        def values(c):
            def pick(rows, n):
                d, i = n // 4, n % 4
                if d:
                    return self.v_back[rows, i, c * C:(c + 1) * C]
                return self.v[rows, i, c * C:(c + 1) * C]
            return pick

        LEVELS = 6
        self.steps = 8 + 3 * (LEVELS - 2) + 2 + 4
        with nc.Block() as block:
            @block.tensor
            def _(pe):
                def need(n):
                    pe.wait_ge(*out.at(n))

                for c in range(chunks):
                    s = c % 2
                    m = {name: pool[name, s] for name in names}
                    A, B, R, K = (cut(x, c) for x in (at, bt, rt, kt))
                    base = c * self.steps
                    need(base)
                    product(0, [(of(A), of(B))])
                    product(1, [(of(B), of(A))])
                    product(2, [(of(B), own)])
                    product(3, [(of(K), own)])
                    product(4, [(values(c), own)])
                    product(5, [(of(K), of(A))])
                    product(6, [(of(B), of(R))])
                    product(7, [(of(K), of(R))])
                    at_step = base + 8
                    for level in range(1, LEVELS):
                        need(at_step)
                        product(0, [(of(m["low"]), of(m["inv"]))])
                        need(at_step + 1)
                        product(1, [(of(m["inv_t"]), of(m["mid"]))])
                        at_step += 2
                        if level < LEVELS - 1:
                            product(2, [(of(m["mid"]), of(m["inv_t"]))])
                            at_step += 1
                    need(at_step)
                    if c == 0:
                        pe.wait_ge(*S("h_ready").at(1))
                    product(3, [(of(A), of(state)), (of(m["ak"]), of(m["v_row"]))])
                    need(at_step + 1)
                    product(4, [(of(m["inv"]), of(m["mid"]))])
                    need(at_step + 2)
                    product(5, [(of(state), of(R)), (of(m["low"]), of(m["rb"])), (of(m["v_row"]), of(m["rk"]))])
                    product(6, [(of(m["b_row"]), of(m["low"])), (of(m["k_row"]), of(m["v_row"]))])

            @block.vector
            def _(dve):
                v = nc.vector
                link = linker(dve, S("dve_step"))
                link(v.memset(self.y, 0.0))
                v.memset(state, 0.0).then_inc(*S("h_ready").up())
                step = 0

                def ready():
                    dve.wait_ge(*done.at(step + 1))

                for c in range(chunks):
                    s = c % 2
                    m = {name: pool[name, s] for name in names}
                    begin = step
                    unit = spread(masks[:, UNIT], 8)
                    whole = self.whole[:, :, :]
                    ready()
                    link(v.tensor_copy(whole, tensors[0]))
                    link(v.tensor_tensor(m["inv_t"], whole, spread(masked(6), 8), ALU.mult))
                    link(v.tensor_tensor(m["low"], whole, spread(masked(7), 8), ALU.mult))
                    v.tensor_tensor(m["inv_t"], m["inv_t"], unit, ALU.add).then_inc(*out.up())
                    step += 1
                    ready()
                    link(v.tensor_tensor(m["inv"], tensors[1], spread(masked(0), 8), ALU.mult))
                    v.tensor_tensor(m["inv"], m["inv"], unit, ALU.add).then_inc(*out.up())
                    step += 1
                    for name, bank in (("b_row", 2), ("k_row", 3), ("v_row", 4)):
                        ready()
                        v.tensor_copy(m[name], tensors[bank]).then_inc(*out.up())
                        step += 1
                    for name, bank, mask in (("ak", 5, STRICT), ("rb", 6, INCL), ("rk", 7, INCL)):
                        ready()
                        v.tensor_tensor(m[name], tensors[bank], spread(masks[:, mask], 8), ALU.mult)\
                            .then_inc(*out.up())
                        step += 1
                    for level in range(1, LEVELS):
                        ready()
                        v.tensor_copy(m["mid"], tensors[0]).then_inc(*out.up())
                        step += 1
                        ready()
                        dve.wait_ge(*out.last())
                        if level < LEVELS - 1:
                            v.tensor_tensor(m["inv"], m["inv"], tensors[1], ALU.add).then_inc(*out.up())
                            step += 1
                            ready()
                            v.tensor_tensor(m["low"], whole, spread(masked(7 + level), 8), ALU.mult)\
                                .then_inc(*S("dve_step").up())
                            v.tensor_tensor(m["inv_t"], m["inv_t"], tensors[2], ALU.add).then_inc(*out.up())
                            step += 1
                        else:
                            v.tensor_tensor(m["inv"], m["inv"], tensors[1], ALU.add).then_inc(*out.up())
                            step += 1
                    ready()
                    v.tensor_copy(m["mid"], tensors[3]).then_inc(*out.up())
                    step += 1
                    ready()
                    v.tensor_copy(m["low"], tensors[4]).then_inc(*out.up())
                    step += 1
                    ready()
                    y = self.y
                    yd = [tensors[5][:, 4 * d:4 * d + 4, :] for d in range(2)]
                    first, second = slice(c * C, (c + 1) * C), slice(T - (c + 1) * C, T - c * C)
                    link(v.tensor_tensor(y[:, :, first], yd[0], y[:, :, first], ALU.add))
                    v.tensor_tensor(y[:, :, second], yd[1][:, :, ::-1], y[:, :, second], ALU.add)\
                        .then_inc(*out.up())
                    step += 1
                    ready()
                    link(v.tensor_tensor(state, state, tensors[6], ALU.add))
                    v.tensor_tensor(state, state, decay_end[:, :, c:c + 1].broadcast_to([P, 8, C]), ALU.mult)\
                        .then_inc(*out.up())
                    step += 1
                    assert step - begin == self.steps
        k.close()

    def finish(self):
        k, y, g = self.k, self.y, self.g
        nc = k.nc
        S = k.counter
        sq, root = (k.ring[:, 8 + i, 0:1024].rearrange("p (n t) -> p n t", n=4) for i in range(2))
        pair = [slice(0, 2), slice(2, 4)]
        sums = [k.bank[i][:, :].rearrange("p (t n) -> p t n", t=2) for i in range(4)]
        with nc.Block() as block:
            @block.tensor
            def _(pe):
                for i in range(2):
                    mm = nc.tensor.matmul(sums[i], k.t("heads2"), y[:, pair[i], :], start=True, stop=True)
                mm.then_inc(*S("sums_ready").up())
                pe.wait_ge(*S("squares_ready").at(1))
                for i in range(2):
                    mm = nc.tensor.matmul(sums[2 + i], k.t("heads2"), sq[:, pair[i], :], start=True, stop=True)
                mm.then_inc(*S("sums_ready").up())

            @block.scalar
            def _(act):
                act.wait_ge(*S("h_ready").at(1))
                nc.scalar.activation(sq, y, ACT.Square).then_inc(*S("squares_ready").up())
                act.wait_ge(*S("var_ready").at(1))
                nc.scalar.activation(root, root, ACT.Sqrt).then_inc(*S("root_ready").up())

            @block.vector
            def _(dve):
                v = nc.vector
                link = linker(dve, S("dve_step"))
                dve.wait_ge(*S("sums_ready").at(1))
                for i in range(2):
                    last = v.scalar_tensor_tensor(y[:, pair[i], :], sums[i], -1.0 / HD, y[:, pair[i], :], ALU.mult,
                                                  ALU.add)
                last.then_inc(*S("h_ready").up())
                dve.wait_ge(*S("sums_ready").at(2))
                for i in range(2):
                    link(v.tensor_scalar(root[:, pair[i], :], sums[2 + i], 1.0 / HD, 64e-5, ALU.mult, ALU.add))
                v.reciprocal(root, root).then_inc(*S("var_ready").up())
                dve.wait_ge(*S("root_ready").at(1))
                link(v.tensor_tensor(y, y, root, ALU.mult))
                for t in range(4):
                    link(v.tensor_scalar(y[:, t, :], y[:, t, :], k.v("gn_w", t), k.v("gn_b", t), ALU.mult, ALU.add))
                link(v.tensor_tensor(y, y, self.bonus, ALU.add))
                link(v.tensor_tensor(y, y, g[:, :, :], ALU.mult))
        k.close()


RUN = None


def program(nc, dram, out):
    with ExitStack() as ctx:
        k = Core(nc, ctx, dram)
        plan = [("ada", 24, RING, 1), ("mix0", 14, RING, 1), ("dense", 42, RING, 1), ("mix1", 14, RING, 1),
                ("moe1", 42, RING, 8), ("hybrid", 32, HYBRID_RING, 1), ("moe2", 12, 12, 16)]
        loads = {}
        for name, n, ring, turns in plan:
            if RUN is None or name in RUN:
                loads[name] = Loads(k.weights, n, ring, turns)
                if name == "ada":
                    k.weights.skipped += 24
            else:
                k.weights.skipped += n * turns
        names = list(loads)

        def after(name):
            at = names.index(name) + 1
            return loads[names[at]] if at < len(names) else Loads(k.weights, 0)

        stage_setup(k, loads["ada"], after("ada"))
        for l in range(2):
            if f"mix{l}" in loads:
                stage_mixer(k, l, loads[f"mix{l}"], after(f"mix{l}"))
            if l == 0 and "dense" in loads:
                stage_dense(k, 0, loads["dense"], after("dense"))
        if "moe1" in loads:
            with ExitStack() as stage:
                m = Mixture(k, stage, "moe1", 8, P, 14, "router1", 8, False,
                            range(HYBRID_RING, RING))
                stage_mixture(k, m, k.amp[:, 1, 1, :], k.mod[:, 1, 24:32], loads["moe1"], after("moe1"),
                              k.mod[:, 1, 40:48])
        if "hybrid" in loads:
            stage_hybrid(k, loads["hybrid"], after("hybrid"))
        if "moe2" in loads:
            with ExitStack() as stage:
                m = Mixture(k, stage, "moe2", 32, C, 2, "router2", 36, True, range(3))
                stage_mixture(k, m, k.v("norm2"), None, loads["moe2"], after("moe2"), None)
        with nc.Block() as block:
            @block.sync
            def _(sp):
                sp.dma_start(out[:, :, :], k.xT[:, :, :]).then_inc(*k.counter("out").up(16))
                sp.wait_ge(*k.counter("out").at(16))


def columns(a, rows=P):
    a = np.asarray(a).reshape(-1)
    n = -(-a.size // P)
    out = np.zeros((n * P,), a.dtype)
    out[:a.size] = a
    return out.reshape(n, P).T


def slots_of(w):
    K, M = w.shape
    return w.reshape(K // P, P, M // T, T).transpose(2, 1, 0, 3).reshape(M // T, P, SLOT)


def ffn_slots(gate, up, down, chunks_per_group):
    E, _, F = gate.shape
    n = F // T
    g, u = (w.reshape(E, DT, P, n, T).transpose(0, 3, 2, 1, 4).reshape(E * n, P, SLOT) for w in (gate, up))
    d = down.reshape(E, n, 2, P, D).transpose(0, 1, 3, 2, 4).reshape(E * n, P, SLOT)
    kinds = {"gate": g, "up": u, "down": d}
    order = chunk_order(chunks_per_group)
    return [(kinds[kind], base + c) for base in range(0, E * n, chunks_per_group) for kind, c in order]


def tables():
    t = np.zeros((P, NTAB), np.float32)
    p = np.arange(P)
    t[:, TAB["ident"]] = np.eye(P)
    t[:, TAB["ones"]] = 1
    t[:, TAB["heads2"]] = (p[:, None] // HD == p[None, :] // HD)
    t[:, TAB["tri"]] = (p[:, None] <= p[None, :])
    rot1 = np.zeros((P, P), np.float32)
    for i in range(16):
        rot1[64 + 16 + i, 64 + i] = -1
        rot1[64 + i, 64 + 16 + i] = 1
    t[:, TAB["rot1"]] = rot1
    rot2 = np.zeros((P, P), np.float32)
    for h in (0, HD):
        for i in range(8):
            rot2[h + 8 + i, h + i] = -1
            rot2[h + i, h + 8 + i] = 1
    t[:, TAB["rot2"]] = rot2
    f1 = np.float32(10000.0) ** (-np.arange(16, dtype=np.float32) / np.float32(16))
    t[64:96, TAB["freq1"].start] = np.tile(f1, 2)
    f2 = np.float32(500000.0) ** (-(np.arange(8, dtype=np.float32) * np.float32(2.0 / 16)))
    t[:, TAB["freq2"].start] = 0
    for h in (0, HD):
        t[h:h + 16, TAB["freq2"].start] = np.tile(f2, 2)
    t[:, TAB["causal"]] = np.where(p[None, :] <= p[:, None], 0, NEG)
    t[:, TAB["iota"]] = p[None, :]
    return t


def recurrence_tables():
    t = np.zeros((P, 1216), np.float32)
    s, u = np.arange(C)[:, None], np.arange(C)[None, :]
    for i in range(6):
        b = 1 << i
        upper = (s // (2 * b) == u // (2 * b)) & (s // b % 2 == 0) & (u // b % 2 == 1)
        t[:, i * C:(i + 1) * C] = np.tile(upper, (2, 1))
        t[:, (6 + i) * C:(7 + i) * C] = np.tile(upper.T, (2, 1))
    t[:, STRICT] = np.tile(s < u, (2, 1))
    t[:, INCL] = np.tile(s <= u, (2, 1))
    t[:, UNIT] = np.tile(s == u, (2, 1))
    t[:, RESET] = (np.arange(T) % C != 0)
    return t


def kernel(**inputs):
    import concourse.bacc as bacc
    from concourse.bass_utils import run_bass_kernel_spmd

    x = {n: np.asarray(a) for n, a in inputs.items()}
    vec = np.zeros((P, NVEC), np.float32)

    def put(name, a):
        cols = columns(a)
        vec[:, VEC[name]] = cols

    for l in range(2):
        for name, key in (("ada_b", "ada_b"), ("attn_g", "attn_norm_g"), ("ffn_g", "ffn_norm_g"),
                          ("q_g", "q_norm_g"), ("kv_g", "kv_norm_g"), ("mla_g", "mla_out_g"),
                          ("fox_g", "fox_out_g"), ("forget_b", "fox_forget_b")):
            put(f"{name}{l}", x[key][l])
    for name, key in (("final_g", "final_norm_g"), ("norm1", "norm1_g_2"), ("norm2", "norm2_g_2"),
                      ("mu_prev", "mu_prev_2"), ("mu_next", "mu_next_2"), ("decay0", "w_decay0_2"),
                      ("gate0", "a_gate0_2"), ("k_k", "k_k_2"), ("k_a", "k_a_2"), ("r_k", "r_k_2"),
                      ("gn_w", "gn_w_2"), ("gn_b", "gn_b_2"), ("b_merge", "b_merge_2")):
        put(name, x[key])
    for name, key in (("qn_g", "q_norm_g_2"), ("kn_g", "k_norm_g_2")):
        put(name, np.tile(x[key].reshape(-1), 2))

    parts = []

    def add(slots):
        parts.extend((slots, i) for i in range(len(slots)))

    for l in range(2):
        add(x["ada_w"][l].T.reshape(24, 2, P, D).transpose(0, 2, 1, 3).reshape(24, P, SLOT))

    def mixer(l):
        w = x["w_in"][l]
        cut = np.cumsum([256, 128, 32, 512, 512, 512, 8])
        cq, ckv, kr, fq, fk, fv, fl = np.split(w, cut[:-1], axis=1)
        misc = np.zeros((D, P), w.dtype)
        misc[:, 0:8] = fl
        misc[:, 64:96] = kr
        add(slots_of(np.concatenate([cq, ckv, misc, fq, fk, fv], axis=1)))
        uq = np.zeros((P, 2, HEADS, P), w.dtype)
        uq[:, :, :, 0:96] = x["w_uq"][l].reshape(2, P, HEADS, 96).transpose(1, 0, 2, 3)
        add(uq.reshape(1, P, SLOT))
        ukv = x["w_ukv"][l].reshape(P, HEADS, 2, HD).transpose(0, 2, 1, 3).reshape(P, 1024)
        add(np.concatenate([ukv, np.zeros_like(ukv)], axis=1).reshape(1, P, SLOT))
        add(slots_of(x["w_o"][l]))

    mixer(0)
    parts.extend(ffn_slots(x["dense_w_gate"], x["dense_w_up"], x["dense_w_down"], FFN_CHUNKS))
    mixer(1)
    more_parts(x, add, parts)
    stream = np.empty((len(parts), P, SLOT), np.float32)
    for i, (a, j) in enumerate(parts):
        stream[i] = a[j]
    arrays = {
        "stream": stream, "vec": vec, "tab": tables(), "c_row": x["c"].reshape(D),
        "xT": np.ascontiguousarray(x["x"][0].T.reshape(DT, P, T).transpose(1, 0, 2)),
        "pos1": x["positions"].reshape(T), "pos2": x["positions_2"].reshape(T),
    }
    arrays.update(more_arrays(x))
    nc = bacc.Bacc("TRN2", target_bir_lowering=False, num_devices=1)
    dram = {n: nc.dram_tensor(n, a.shape, mybir.dt.from_np(a.dtype), kind="ExternalInput").ap()
            for n, a in arrays.items()}
    out = nc.dram_tensor("out", (P, DT, T), F32, kind="ExternalOutput").ap()
    program(nc, dram, out)
    got = run_bass_kernel_spmd(nc, [arrays], core_ids=[0]).results[0]["out"]
    return np.ascontiguousarray(got.transpose(2, 1, 0).reshape(1, T, D))


def more_parts(x, add, parts):
    parts.extend(ffn_slots(x["moe_w_gate"][0], x["moe_w_up"][0], x["moe_w_down"][0], 14))
    w = x["w_in_2"][0]
    add(slots_of(w))
    lora = np.zeros((P, SLOT), w.dtype)
    for d in range(2):
        lora[0:64, d * 512:(d + 1) * 512] = x["w_decay_up_2"][0, d]
        lora[64:128, d * 512:(d + 1) * 512] = x["a_gate_up_2"][0, d]
    lora[:, 1024:1536] = x["g_up_2"][0]
    add(x["w_attn_out_2"][0].reshape(1, 2, P, D).transpose(0, 2, 1, 3).reshape(1, P, SLOT))
    add(lora[None])
    add(x["w_rwkv_out_2"][0].reshape(4, P, 2, 512).transpose(2, 1, 0, 3).reshape(2, P, SLOT))
    add(slots_of(x["w_out_2"][0]))
    parts.extend(ffn_slots(x["w_gate_2"][0], x["w_up_2"][0], x["w_down_2"][0], 4))


def more_arrays(x):
    def router(w):
        return np.ascontiguousarray(w.reshape(DT, P, -1).transpose(1, 0, 2))
    q, key = np.arange(T)[:, None], np.arange(T)[None, :]
    windows = (abs(q - key) <= 64, (q - key) % 4 == 0, (q - key) % 16 == 0)
    dilated = np.stack([np.where(w, 0, NEG) for w in windows], 1).reshape(TT, P, 3 * T).transpose(1, 0, 2)
    return {"tab2": recurrence_tables(), "dilated": np.ascontiguousarray(dilated, np.float32), "router1": router(x["router_w"][0]),
            "router2": router(np.concatenate([x["w_router_group_2"][0], x["w_router_expert_2"][0]], axis=1)),
            "router_b": np.concatenate([x["b_router_group_2"][0], x["b_router_expert_2"][0]])}
```
